# Optimizing a Trainium2 kernel written in Bass

```python
import jax, jax.numpy as jnp
from jax import lax
import numpy as np

D_MODEL = 1024
BATCH = 1
SEQ = 512
DEPTH = 1

MIX_WIDTH = D_MODEL
CONV_WIDTH = MIX_WIDTH // 2
CONV_HEADS = 8
POOL_WIDTH = MIX_WIDTH - CONV_WIDTH
CONV_K = 3
POOL_WINDOWS = (2, 4, 8, 16)
N_POOL_GROUPS = len(POOL_WINDOWS)
POOL_GROUP = POOL_WIDTH // N_POOL_GROUPS
IN_COLS = 3 * CONV_WIDTH + POOL_WIDTH
N_EXPERTS = 16
N_EXPERT_GROUPS = 4
EXPERTS_PER_GROUP = N_EXPERTS // N_EXPERT_GROUPS
TOP_K = 2
D_EXPERT = D_MODEL // 2
EPS = 1e-6

kernel_name = "hybrid_conv_pool_grouped_moe_block"

def rmsnorm(x, g):
    xf = x.astype(jnp.float32)
    y = xf * lax.rsqrt(jnp.mean(xf * xf, axis=-1, keepdims=True) + EPS)
    return (y * g.astype(jnp.float32)).astype(x.dtype)

def modulate(h, shift, scale):
    return h * (1.0 + scale) + shift

def short_gated_conv(u_b, u_c, u_h, w):
    g = u_c * u_h
    gp = jnp.pad(g, ((0, 0), (CONV_K - 1, 0), (0, 0)))
    s = g.shape[1]
    conv = w[0] * gp[:, 0:s] + w[1] * gp[:, 1:s + 1] + w[2] * gp[:, 2:s + 2]
    return u_b * conv

def multiscale_pool(v, pool_w, pool_scale):
    s = v.shape[1]
    vf = v.astype(jnp.float32)
    cs = jnp.cumsum(vf, axis=1)
    t = jnp.arange(1, s + 1)
    groups = []
    for gi, win in enumerate(POOL_WINDOWS):
        sl = slice(gi * POOL_GROUP, (gi + 1) * POOL_GROUP)
        cs_g = cs[..., sl]
        lag = jnp.pad(cs_g, ((0, 0), (win, 0), (0, 0)))[:, :s]
        cnt = jnp.minimum(t, win).astype(jnp.float32)[:, None]
        groups.append((cs_g - lag) / cnt - vf[..., sl])
    pooled = jnp.stack(groups, axis=2).astype(v.dtype)
    y = jnp.einsum('bsgc,gcd->bsgd', pooled, pool_w)
    y = y.reshape(v.shape[0], s, POOL_WIDTH)
    return y * pool_scale

def route(h, w_router, router_bias):
    logits = jnp.einsum('bsd,de->bse', h, w_router).astype(jnp.float32)
    s = jax.nn.sigmoid(logits)
    sel = s + router_bias.astype(jnp.float32)
    sel_g = sel.reshape(*sel.shape[:-1], N_EXPERT_GROUPS, EXPERTS_PER_GROUP)
    gscore = lax.top_k(sel_g, TOP_K)[0].sum(-1)
    best = jnp.argmax(gscore, axis=-1)
    in_group = (jnp.arange(N_EXPERTS) // EXPERTS_PER_GROUP) == best[..., None]
    masked = jnp.where(in_group, sel, -jnp.inf)
    _, idx = lax.top_k(masked, TOP_K)
    w = jnp.take_along_axis(s, idx, axis=-1)
    w = w / jnp.sum(w, axis=-1, keepdims=True)
    combine = jnp.sum(jax.nn.one_hot(idx, N_EXPERTS, dtype=jnp.float32) * w[..., None], axis=-2)
    return combine

def moe(h, w_router, router_bias, w_gate_up, w_down):
    combine = route(h, w_router, router_bias).astype(h.dtype)
    out = jnp.zeros_like(h)
    for e in range(N_EXPERTS):
        gu = jnp.einsum('bsd,df->bsf', h, w_gate_up[e])
        g, u = jnp.split(gu, 2, axis=-1)
        y = jnp.einsum('bsf,fd->bsd', jax.nn.silu(g) * u, w_down[e])
        out = out + combine[..., e:e + 1] * y
    return out

def setup_inputs(seed: int = 0) -> dict:
    key = jax.random.key(seed)
    ks = jax.random.split(key, 20)
    f32 = jnp.float32
    d = D_MODEL
    nrm = lambda k, shape, sc: jax.random.normal(k, shape, f32) * sc
    return {
        "x": nrm(ks[0], (BATCH, SEQ, d), 1.0),
        "c": nrm(ks[1], (BATCH, d), 1.0),
        "w_in": nrm(ks[2], (DEPTH, d, IN_COLS), d ** -0.5),
        "conv_w": nrm(ks[3], (DEPTH, CONV_K, CONV_WIDTH), CONV_K ** -0.5),
        "pool_w": nrm(ks[4], (DEPTH, N_POOL_GROUPS, POOL_GROUP, POOL_GROUP), POOL_GROUP ** -0.5),
        "pool_scale": 1.0 + nrm(ks[5], (DEPTH, POOL_WIDTH), 0.1),
        "w_out": nrm(ks[6], (DEPTH, MIX_WIDTH, d), MIX_WIDTH ** -0.5),
        "norm1_g": 1.0 + nrm(ks[7], (DEPTH, d), 0.05),
        "norm2_g": 1.0 + nrm(ks[8], (DEPTH, d), 0.05),
        "w_ada": nrm(ks[9], (DEPTH, d, 6 * d), 0.5 * d ** -0.5),
        "b_ada": nrm(ks[10], (DEPTH, 6 * d), 0.02),
        "w_router": nrm(ks[11], (d, N_EXPERTS), d ** -0.5),
        "router_bias": nrm(ks[12], (N_EXPERTS,), 0.01),
        "w_gate_up": nrm(ks[13], (DEPTH, N_EXPERTS, d, 2 * D_EXPERT), d ** -0.5),
        "w_down": nrm(ks[14], (DEPTH, N_EXPERTS, D_EXPERT, d), D_EXPERT ** -0.5),
        "final_g": 1.0 + nrm(ks[15], (d,), 0.05),
    }

def reference(x, c, w_in, conv_w, pool_w, pool_scale, w_out, norm1_g, norm2_g,
              w_ada, b_ada, w_router, router_bias, w_gate_up, w_down, final_g):
    c_act = jax.nn.silu(c)
    for l in range(DEPTH):
        mod = jnp.einsum('bd,de->be', c_act, w_ada[l]) + b_ada[l]
        sh1, sc1, g1, sh2, sc2, g2 = [m[:, None, :] for m in jnp.split(mod, 6, axis=-1)]

        h = modulate(rmsnorm(x, norm1_g[l]), sh1, sc1)
        proj = jnp.einsum('bsd,de->bse', h, w_in[l])
        u_b = proj[..., 0:CONV_WIDTH]
        u_c = proj[..., CONV_WIDTH:2 * CONV_WIDTH]
        u_h = proj[..., 2 * CONV_WIDTH:3 * CONV_WIDTH]
        v = proj[..., 3 * CONV_WIDTH:]
        y_conv = short_gated_conv(u_b, u_c, u_h, conv_w[l])
        y_pool = multiscale_pool(v, pool_w[l], pool_scale[l])
        y_mix = jnp.concatenate([y_conv, y_pool], axis=-1)
        x = x + g1 * jnp.einsum('bse,ed->bsd', y_mix, w_out[l])

        h2 = modulate(rmsnorm(x, norm2_g[l]), sh2, sc2)
        x = x + g2 * moe(h2, w_router, router_bias, w_gate_up[l], w_down[l])
    return rmsnorm(x, final_g)


_drawn_inputs = setup_inputs


def setup_inputs(seed=0):
    import zlib

    import numpy as np

    out = dict(_drawn_inputs(seed))
    spreads = {}
    factors = {}
    for name, (base, spread) in spreads.items():
        noise = np.random.default_rng([zlib.crc32(name.encode()), seed]).standard_normal(out[name].shape)
        drawn = base * np.exp(spread * noise) if base else spread * noise
        out[name] = __import__('jax').numpy.asarray(drawn.astype(out[name].dtype))
    for name, factor in factors.items():
        out[name] = (out[name] * factor).astype(out[name].dtype)
    return out
```

```python
from contextlib import ExitStack

import concourse.bass as bass
from concourse import mybir

F32 = mybir.dt.float32
BF16 = mybir.dt.bfloat16
U32 = mybir.dt.uint32
I32 = mybir.dt.int32
ALU = mybir.AluOpType
ACT = mybir.ActivationFunctionType
AX_X = mybir.AxisListType.X

P = 128
EPS = 1e-6
BIG = 1e30


def hybrid_block(nc, x, c, w_in, conv_w, pool_w, pool_scale, w_out, norm1_g, norm2_g,
                 w_ada, b_ada, w_router, router_bias, w_gate_up, w_down, final_g, out):
    T, D = x.shape[1], x.shape[2]
    NT, KD = T // P, D // P
    CW = conv_w.shape[2]
    NC = CW // P
    NG = pool_w.shape[1]
    WINDOWS = [2 << g for g in range(NG)]
    PAD = WINDOWS[-1]
    TAPS = conv_w.shape[1]
    E = w_router.shape[1]
    GRP = 4
    EG = E // GRP
    F = w_down.shape[2]
    KF = F // P
    HALF = D // 2
    PIECE = 4 * D
    MAIN = E * P
    MOST_OVER = 2 * T // P - 1

    ctx = ExitStack()
    with ctx:
        def sb(name, shape, dt=F32):
            return ctx.enter_context(nc.sbuf_tensor(name, shape, dt))

        def sem(name):
            return ctx.enter_context(nc.semaphore(name))

        bank = [ctx.enter_context(nc.psum_tensor(f"bank{i}", [P, HALF], F32)) for i in range(8)]

        ring = sb("ring", [P, 6, PIECE])
        wout = sb("wout", [P, 2 * PIECE])
        x_sb = sb("x_sb", [P, NT, D])
        hT = sb("hT", [P, KD, T])
        yT = sb("yT", [P, KD, T])
        acc = sb("acc", [P, 2, D])
        gate_bc = sb("gate_bc", [P, D])
        scale2_bc = sb("scale2_bc", [P, D])
        shift2_bc = sb("shift2_bc", [P, D])
        mixbuf = sb("mixbuf", [P, 4 * (PAD + T)])
        ident = sb("ident", [P, P])
        ones = sb("ones", [P, P])
        before = sb("before", [P, P], BF16)
        ones_h = sb("ones_h", [P, P], BF16)
        prm = sb("prm", [32, P])
        prmT = sb("prmT", [P, 32])
        c_act = sb("c_act", [P, KD])
        mod1 = sb("mod1", [P, 2, KD])
        icnt = sb("icnt", [P, PAD])
        stat = sb("stat", [P, 4, NT])
        wr = sb("wr", [P, KD, E])
        bias_bc = sb("bias_bc", [P, E])
        iota_j = sb("iota_j", [P, P], BF16)
        tok_id = sb("tok_id", [P, NT, 2], BF16)
        iota_e = sb("iota_e", [P, E])
        desc = sb("desc", [P, GRP])
        idx_main = sb("idx_main", [P, E], U32)
        idx_over = sb("idx_over", [P, 1], U32)
        slot_u = sb("slot_u", [P, 2, NT], U32)
        over_n = sb("over_n", [P, 2], I32)

        vpad, sum_a, sum_b, gpad = (mixbuf[:, i * (PAD + T):(i + 1) * (PAD + T)] for i in range(4))
        route = [mixbuf[:, i * NT * E:(i + 1) * NT * E] for i in range(22)]
        tail = mixbuf[:, 22 * NT * E:]
        combine = tail[:, 0:2 * NT].rearrange("p (i t) -> p i t", i=2)
        over_rel = tail[:, 2 * NT:4 * NT].rearrange("p (i t) -> p i t", i=2)
        over_sum, over_cmp = tail[:, E:2 * E], tail[:, 2 * E:3 * E]
        over_k, over_e = tail[:, 3 * E:3 * E + 1], tail[:, 3 * E + 1:3 * E + 2]

        onehot = wout[:, 0:2 * T * E // 4].bitcast(BF16).rearrange("p (t e j) -> p t e j", t=NT, e=E)
        xg = [wout[:, PIECE + i * D:PIECE + (i + 1) * D] for i in range(2)]
        y_sb = [wout[:, PIECE + (2 + i) * D:PIECE + (3 + i) * D] for i in range(2)]
        yflat = yT[:, :, :].rearrange("p k t -> p (k t)")
        xselT = yflat[:, 0:D].rearrange("p (k j) -> p k j", k=KD)
        silu_g = yflat[:, D:D + F]
        hid = yflat[:, D + F:D + 2 * F]
        hidT = yflat[:, 2 * D:2 * D + F].rearrange("p (k j) -> p k j", k=KF)
        over_hot = yflat[:, 3 * D:3 * D + NT * P // 2].bitcast(BF16).rearrange("p (t j) -> p t j", t=NT)
        hflat = hT[:, :, :].rearrange("p k t -> p (k t)")
        h2 = [hflat[:, t * D:(t + 1) * D] for t in range(NT)]
        final_bc = h2[0]
        h2T = acc[:, 0, :].rearrange("p (k j) -> p k j", k=KD)
        pool_w_sb = wout[:, 0:NG * P].rearrange("p (g d) -> p g d", g=NG)
        wout_sb = wout[:, :].rearrange("p (k n) -> p k n", k=KD)
        ring_k = [ring[:, s, :].rearrange("p (k n) -> p k n", k=4) for s in range(6)]
        ring_w = [ring[:, s, :].rearrange("p (k n) -> p k n", k=KD) for s in range(6)]
        ring_flat = ring[:, :, :].rearrange("p s n -> p (s n)")
        ya = [ring_flat[:, t * D:(t + 1) * D] for t in range(NT)]
        yb = [ring_flat[:, (NT + t) * D:(NT + t + 1) * D] for t in range(NT)]
        res = [ring_flat[:, (2 * NT + t) * D:(2 * NT + t + 1) * D] for t in range(NT)]

        h2_dram = nc.dram_tensor("h2_rows", [T, D], F32)
        y_dram = nc.dram_tensor("y_rows", [MAIN + MOST_OVER * P, D], F32)

        prm_in, wr_in, bias_in, poolw_in, norm2_in, final_in = (
            sem(n) for n in ("prm_in", "wr_in", "bias_in", "poolw_in", "norm2_in", "final_in"))
        ada1_in = [sem(f"ada1_in{i}") for i in range(8)]
        x_in = sem("x_in")
        win_in = [sem(f"win_in{i}") for i in range(4)]
        ada2_in = [sem(f"ada2_in{i}") for i in range(8)]
        wout_in = sem("wout_in")
        slot_in = [sem(f"slot_in{i}") for i in range(6)]
        brow_in = [sem(f"brow_in{i}") for i in range(6)]
        const_ok, acc_zero, pads_ok, pool_order = (sem(n) for n in ("const_ok", "acc_zero", "pads_ok", "pool_order"))
        prmT_pe, prmT_ok, cact_ok, ada_ok, acc_used = (
            sem(n) for n in ("prmT_pe", "prmT_ok", "cact_ok", "ada_ok", "acc_used"))
        sq_ok, ms_ok, root_ok, rstd_ok, xn_ok, xT_pe, xT_ok = (
            sem(n) for n in ("sq_ok", "ms_ok", "root_ok", "rstd_ok", "xn_ok", "xT_pe", "xT_ok"))
        mod1_ok, hT_act, hT_dve, proj_pe, act_ev, dve_ev = (
            sem(n) for n in ("mod1_ok", "hT_act", "hT_dve", "proj_pe", "act_ev", "dve_ev"))
        pooled_ok, pool_pe, pool_ev, conv_ok, bc_pe, bc_ev, shift_ok, scale_ok = (
            sem(n) for n in ("pooled_ok", "pool_pe", "pool_ev", "conv_ok", "bc_pe", "bc_ev", "shift_ok", "scale_ok"))
        mix_pe, x2_ok, sq2_ok, ms2_ok, root2_ok, rstd2_ok, xn2_ok, h2_ok = (
            sem(n) for n in ("mix_pe", "x2_ok", "sq2_ok", "ms2_ok", "root2_ok", "rstd2_ok", "xn2_ok", "h2_ok"))
        h2T_pe, h2T_ok, logit_pe, score_ok, h2_stored = (
            sem(n) for n in ("h2T_pe", "h2T_ok", "logit_pe", "score_ok", "h2_stored"))
        mask_ok, rank_pe, rank_ev, hot_ok, idx_pe, idx_ok, slots_ok, over_ok = (
            sem(n) for n in ("mask_ok", "rank_pe", "rank_ev", "hot_ok", "idx_pe", "idx_ok", "slots_ok", "over_ok"))
        gate2_pe, gate2_ok = sem("gate2_pe"), sem("gate2_ok")
        icnt_ok, filled = sem("icnt_ok"), sem("filled")
        order = sem("vector_order")
        gathered = [sem("gathered0"), sem("gathered1")]
        stored = [sem("stored0"), sem("stored1")]
        half_pe, sel_pe, sel_ok, gu_pe, silu_ok, hid_ok, hidT_pe, hidT_ok, y_pe, y_ok = (
            sem(n) for n in ("half_pe", "sel_pe", "sel_ok", "gu_pe", "silu_ok", "hid_ok", "hidT_pe",
                             "hidT_ok", "y_pe", "y_ok"))
        o_pick, o_idx_pe, o_idx, o_sel_pe, o_sel, o_w, o_gu, o_silu, o_hid, o_hidT_pe, o_hidT, o_y_pe, o_y = (
            sem("over_" + n) for n in ("pick", "idx_pe", "idx", "sel_pe", "sel", "w", "gu", "silu",
                                       "hid", "hidT_pe", "hidT", "y_pe", "y"))
        o_gathered, o_stored, o_order, o_seen = (sem("over_" + n) for n in ("gathered", "stored", "order", "seen"))
        all_rows, fin_rstd, fin_stat, fin_sq, fin_root, res_ok, out_in = (
            sem(n) for n in ("all_rows", "fin_rstd", "fin_stat", "fin_sq", "fin_root", "res_ok", "out_in"))
        tok_in = [sem(f"tok_in{t}") for t in range(NT)]

        tiles = [("v", g) for g in range(NG)] + [(m, i) for i in range(NC) for m in ("C", "h", "B")]
        GROUP = {"B": 0, "C": 1, "h": 2, "v": 3}
        WSLOT = {"v": 4, "C": 5, "h": 0, "B": 1}
        WORDER = ["v", "C", "h", "B"]
        n_act = n_dve = 0
        freed = []
        for m, _ in tiles:
            if m in ("v", "C"):
                n_act += 1
                freed.append((act_ev, n_act))
            else:
                n_dve += 1
                freed.append((dve_ev, n_dve))
        ADA_SLOTS = [(0, 1), (2, 3), (2, 3), (4, 2), (3, 4), (2, 3)]
        REDUCE_AFTER = {9: 2, 11: 3, 14: 4}
        ADA_FROM, ADA_PER = 4, 3

        block = ctx.enter_context(nc.Block())
        LOOP = 3
        STEPS_OVER = 2 * NT + 4

        @block.sync
        def _(sp):
            def ada(j, half, to, signals, ks):
                src = w_ada[0, half * 4 * P:(half * 4 + 4) * P, j * D:(j + 1) * D].rearrange("(k p) n -> p k n", p=P)
                for q in range(0, 4, ks):
                    sp.dma_start(ring_k[to][:, q:q + ks, :], src[:, q:q + ks, :]).then_inc(signals[q // ks], 16)

            ada(0, 0, 0, ada1_in[0:2], 2)
            sp.dma_start(x_sb[:, :, :], x[0].rearrange("(t p) d -> p t d", p=P)).then_inc(x_in, 16)
            ada(0, 1, 1, ada1_in[2:4], 2)
            ada(1, 0, 2, ada1_in[4:6], 2)
            ada(1, 1, 3, ada1_in[6:8], 2)
            for n, m in enumerate(WORDER):
                if m == "h":
                    sp.wait_ge(ada_ok, 4)
                if m == "B":
                    sp.wait_ge(ada_ok, 8)
                g = GROUP[m]
                sp.dma_start(ring_w[WSLOT[m]][:, :, :],
                             w_in[0, :, g * CW:(g + 1) * CW].rearrange("(k p) n -> p k n", p=P)).then_inc(win_in[n], 16)
            for j in range(2, 6):
                for half in range(2):
                    n = 2 * (j - 2) + half
                    if n == 2:
                        sp.wait_ge(proj_pe, NG)
                    else:
                        sp.wait_ge(ada_ok, {0: 12, 1: 16}.get(n, 4 * (n + 2)))
                    ada(j, half, ADA_SLOTS[j][half], [ada2_in[n]], 4)
            for lo in range(0, MOST_OVER, NT):
                n = min(NT, MOST_OVER - lo)
                sp.dma_start(y_dram[MAIN + lo * P:MAIN + (lo + n) * P, :].rearrange("(t p) d -> p t d", p=P),
                             x_sb[:, 0:n, :]).then_inc(filled, 16)
            sp.wait_ge(pool_pe, NG)
            sp.dma_start(wout_sb, w_out[0].rearrange("(k p) n -> p k n", p=P)).then_inc(wout_in, 16)

            def gate_up(e, half, to):
                src = w_gate_up[0, bass.ds(e, 1), half * 4 * P:(half * 4 + 4) * P, :]
                sp.dma_start(ring_k[to][:, :, :], src.rearrange("a (k p) n -> p (a k) n", p=P)).then_inc(slot_in[to], 16)

            def down(e, to):
                src = w_down[0, bass.ds(e, 1)]
                sp.dma_start(ring_k[to][:, :, :], src.rearrange("a (k p) n -> p (a k) n", p=P)).then_inc(slot_in[to], 16)

            sp.wait_ge(ada_ok, 40)
            gate_up(0, 0, 4)
            sp.wait_ge(proj_pe, len(tiles))
            gate_up(0, 1, 5)
            gate_up(1, 0, 0)
            gate_up(1, 1, 1)
            sp.wait_ge(ada_ok, 44)
            down(0, 2)
            sp.wait_ge(ada_ok, 48)
            gate_up(2, 0, 3)
            sp.wait_ge(half_pe, 1)
            gate_up(2, 1, 4)
            sp.wait_ge(gu_pe, 1)
            down(1, 5)

            def refill(e, s):
                sp.wait_ge(half_pe, e - 1)
                gate_up(e, 0, s)
                sp.wait_ge(gu_pe, e - 1)
                gate_up(e, 1, s + 1)
                sp.wait_ge(y_pe, e - 2)
                down(e - 1, s + 2)

            with sp.Fori(LOOP, E - 1, 2) as e:
                refill(e, 0)
                refill(e + 1, 3)
            refill(E - 1, 0)
            sp.wait_ge(y_pe, E - 2)
            down(E - 1, 5)

            sp.wait_ge(over_ok, 1)
            n_over = sp.value_load(over_n[0:1, 0:1], min_val=0, max_val=MOST_OVER)
            sp.wait_ge(y_pe, E)
            with sp.If(n_over > 0):
                with sp.Fori(0, n_over) as o:
                    sp.wait_ge(o_pick, o + 1)
                    sp.sem_inc(o_seen, 1)
                    ex = sp.value_load(over_n[0:1, 1:2], min_val=0, max_val=E - 1)
                    for half in range(2):
                        src = w_gate_up[0, bass.ds(ex, 1), half * 4 * P:(half * 4 + 4) * P, :]
                        sp.dma_start(ring_k[half][:, :, :], src.rearrange("a (k p) n -> p (a k) n", p=P)).then_inc(o_w, 16)
                    sp.dma_start(ring_k[2][:, :, :],
                                 w_down[0, bass.ds(ex, 1)].rearrange("a (k p) n -> p (a k) n", p=P)).then_inc(o_w, 16)

            for t in range(NT):
                sp.wait_ge(res_ok, t + 1)
                sp.dma_start(out[0, t * P:(t + 1) * P, :], res[t]).then_inc(out_in, 16)
            sp.wait_ge(out_in, 16 * NT)

        @block.gpsimd
        def _(pool):
            nc.gpsimd.memset(ident[:], 0.0).then_inc(pool_order, 1)
            nc.gpsimd.memset(acc[:, 0, :], 0.0).then_inc(acc_zero, 1)
            pool.wait_ge(pool_order, 1)
            nc.gpsimd.affine_select(out=ident[:], in_=ident[:], compare_op=ALU.not_equal, fill=1.0, base=0,
                                    pattern=[[-1, P]], channel_multiplier=1).then_inc(const_ok, 1)
            nc.gpsimd.memset(acc[:, 1, :], 0.0).then_inc(acc_zero, 1)
            for j in range(2):
                pool.wait_ge(acc_zero, j + 1)
                pool.dma_start(acc[0:1, j, :], b_ada[:, j * D:(j + 1) * D]).then_inc(brow_in[j], 16)
            nc.gpsimd.memset(ones[:], 1.0).then_inc(const_ok, 1)
            nc.gpsimd.memset(vpad[:, 0:PAD], 0.0).then_inc(pads_ok, 1)
            nc.gpsimd.memset(gpad[:, 0:TAPS - 1], 0.0).then_inc(pads_ok, 1)
            iota = lambda to, pattern, base, step: nc.gpsimd.iota(
                to, pattern=pattern, base=base, channel_multiplier=step, allow_small_or_imprecise_dtypes=True)
            iota(icnt[:], [[1, PAD]], 1, 0).then_inc(pads_ok, 1)
            nc.gpsimd.memset(before[:], 1.0).then_inc(pool_order, 1)
            pool.wait_ge(pool_order, 2)
            nc.gpsimd.affine_select(out=before[:], in_=before[:], compare_op=ALU.is_gt, fill=0.0, base=0,
                                    pattern=[[1, P]], channel_multiplier=-1).then_inc(const_ok, 1)
            nc.gpsimd.memset(ones_h[:], 1.0).then_inc(const_ok, 1)
            iota(iota_j[:], [[1, P]], 0, 0).then_inc(const_ok, 1)
            iota(iota_e[:], [[1, E]], 0, 0).then_inc(const_ok, 1)
            iota(desc[:], [[-1, GRP]], GRP, 0).then_inc(const_ok, 1)
            iota(tok_id[:, :, 0], [[0, NT]], 0, 1).then_inc(const_ok, 1)
            iota(tok_id[:, :, 1], [[P, NT]], 0, 0).then_inc(const_ok, 1)
            for j in range(2, 6):
                pool.wait_ge(*((acc_used, j - 1) if j < 4 else (bc_pe, j - 3)))
                nc.gpsimd.memset(acc[:, j % 2, :], 0.0).then_inc(acc_zero, 1)
                pool.wait_ge(acc_zero, j + 1)
                pool.dma_start(acc[0:1, j % 2, :], b_ada[:, j * D:(j + 1) * D]).then_inc(brow_in[j], 16)
            for t in range(NT):
                pool.wait_ge(h2_ok, t + 1)
                pool.dma_start(h2_dram[t * P:(t + 1) * P, :], h2[t]).then_inc(h2_stored, 16)
            pool.wait_ge(h2_stored, 16 * NT)

            def gather(idx, to, signal):
                pool.indirect_dma_start(out=to, out_offset=None, in_=h2_dram[:, :],
                                        in_offset=bass.IndirectOffsetOnAxis(ap=idx, axis=0)).then_inc(signal, 16)

            for e in range(2):
                pool.wait_ge(idx_ok, 1)
                gather(idx_main[:, e:e + 1], xg[e], gathered[e])
            for e in range(E):
                if e + 2 < E:
                    if (e + 2) % GRP == 0:
                        pool.wait_ge(idx_ok, (e + 2) // GRP + 1)
                    pool.wait_ge(sel_pe, e + 1)
                    gather(idx_main[:, e + 2:e + 3], xg[e % 2], gathered[e % 2])
                pool.wait_ge(y_ok, 2 * (e + 1))
                pool.dma_start(y_dram[e * P:(e + 1) * P, :], y_sb[e % 2]).then_inc(stored[e % 2], 16)

            pool.wait_ge(over_ok, 1)
            n_over = pool.value_load(over_n[0:1, 0:1], min_val=0, max_val=MOST_OVER)
            for i in range(2):
                pool.wait_ge(stored[i], 16 * (E // 2))
            with pool.If(n_over > 0):
                with pool.Fori(0, n_over) as o:
                    pool.wait_ge(o_idx, o + 1)
                    pool.sem_inc(o_seen, 1)
                    gather(idx_over[:, 0:1], xg[0], o_gathered)
                    pool.wait_ge(o_y, 2 * o + 2)
                    pool.dma_start(y_dram[bass.ds(MAIN + o * P, P), :], y_sb[0]).then_inc(o_stored, 16)
                    pool.wait_ge(o_stored, 16 * o + 16)
            pool.wait_ge(slots_ok, 1)
            for t in range(NT):
                for i, to in enumerate((ya[t], yb[t])):
                    pool.indirect_dma_start(out=to, out_offset=None, in_=y_dram[:, :],
                                            in_offset=bass.IndirectOffsetOnAxis(ap=slot_u[:, i, t:t + 1], axis=0)
                                            ).then_inc(tok_in[t], 16)

        @block.scalar
        def _(act):
            rows = 2 * KD
            act.dma_start(prm[0:KD, :], c.rearrange("b (k p) -> (b k) p", p=P)).then_inc(prm_in, 16)
            act.dma_start(prm[KD:rows, :], norm1_g.rearrange("b (k p) -> (b k) p", p=P)).then_inc(prm_in, 16)
            act.dma_start(prm[rows:rows + TAPS * NC, :],
                          conv_w.rearrange("l k (i p) -> (l k i) p", p=P)).then_inc(prm_in, 16)
            act.dma_start(prm[rows + TAPS * NC:32, :], pool_scale.rearrange("l (i p) -> (l i) p", p=P)).then_inc(prm_in, 16)
            act.dma_start(pool_w_sb, pool_w[0].rearrange("g c d -> c g d")).then_inc(poolw_in, 16)
            act.dma_start(wr[:, :, :], w_router.rearrange("(k p) e -> p k e", p=P)).then_inc(wr_in, 16)
            act.dma_start(bias_bc[:, :], router_bias.rearrange("(a e) -> a e", a=1).to_broadcast([P, E])).then_inc(bias_in, 16)
            act.dma_start(scale2_bc[:, :], norm2_g.to_broadcast([P, D])).then_inc(norm2_in, 16)

            act.wait_ge(prmT_ok, 1)
            nc.scalar.activation(c_act[:], prmT[:, 0:KD], ACT.Silu).then_inc(cact_ok, 1)
            act.wait_ge(x_in, 16)
            for t in range(NT):
                nc.scalar.activation(yflat[:, t * D:(t + 1) * D], x_sb[:, t, :], ACT.Square,
                                     accum_out=stat[:, 0, t:t + 1]).then_inc(sq_ok, 1)
            act.wait_ge(ms_ok, 1)
            nc.scalar.activation(stat[:, 1, :], stat[:, 3, :], ACT.Sqrt).then_inc(root_ok, 1)
            act.wait_ge(rstd_ok, 1)
            act.wait_ge(sq_ok, NT)
            for t in range(NT):
                nc.scalar.activation(yflat[:, t * D:(t + 1) * D], x_sb[:, t, :], ACT.Copy,
                                     scale=stat[:, 2, t:t + 1]).then_inc(xn_ok, 1)
            for k in range(KD):
                act.wait_ge(xT_pe, k + 1)
                nc.scalar.activation(hT[:, k, :], bank[k][:], ACT.Copy).then_inc(xT_ok, 1)
            act.wait_ge(mod1_ok, 2)
            act.wait_ge(xT_ok, KD)
            for k in range(1, KD, 2):
                nc.scalar.activation(hT[:, k, :], hT[:, k, :], ACT.Identity, scale=mod1[:, 1, k:k + 1],
                                     bias=mod1[:, 0, k:k + 1]).then_inc(hT_act, 1)

            for n, (m, i) in enumerate(tiles):
                if m == "v":
                    act.wait_ge(proj_pe, n + 1)
                    if i == 0:
                        act.wait_ge(pads_ok, 3)
                    else:
                        act.wait_ge(pooled_ok, i)
                    nc.scalar.activation(vpad[:, PAD:], bank[n % 4][:], ACT.Copy).then_inc(act_ev, 1)
                if m == "C":
                    if i == 0:
                        act.wait_ge(pooled_ok, NG)
                    else:
                        act.wait_ge(dve_ev, 2 * i - 1)
                    act.wait_ge(proj_pe, n + 1)
                    nc.scalar.activation(sum_a[:, 0:T], bank[n % 4][:], ACT.Copy).then_inc(act_ev, 1)
                if 1 <= n <= NG:
                    g = n - 1
                    act.wait_ge(pool_pe, g + 1)
                    o = rows + TAPS * NC + g
                    nc.scalar.activation(yT[:, NC + g, :], bank[4 + g % 2][:], ACT.Copy,
                                         scale=prmT[:, o:o + 1]).then_inc(pool_ev, 1)
                j = REDUCE_AFTER.get(n)
                if j in (2, 3):
                    act.wait_ge(bc_pe, j - 1)
                    for h in range(2):
                        nc.scalar.activation((gate_bc if j == 2 else shift2_bc)[:, h * HALF:(h + 1) * HALF],
                                             bank[6 + h][:], ACT.Copy).then_inc(bc_ev, 1)

            for t in range(NT):
                act.wait_ge(x2_ok, t + 1)
                nc.scalar.activation(h2[t], x_sb[:, t, :], ACT.Square, accum_out=stat[:, 0, t:t + 1]).then_inc(sq2_ok, 1)
                act.wait_ge(ms2_ok, t + 1)
                nc.scalar.activation(stat[:, 1, t:t + 1], stat[:, 3, t:t + 1], ACT.Sqrt).then_inc(root2_ok, 1)
                act.wait_ge(rstd2_ok, t + 1)
                act.wait_ge(sq2_ok, t + 1)
                nc.scalar.activation(h2[t], x_sb[:, t, :], ACT.Copy, scale=stat[:, 2, t:t + 1]).then_inc(xn2_ok, 1)
                if t == NT - 1:
                    act.wait_ge(gate2_pe, 1)
                    for h in range(2):
                        nc.scalar.activation(gate_bc[:, h * HALF:(h + 1) * HALF], bank[h][:], ACT.Copy).then_inc(gate2_ok, 1)
                act.wait_ge(h2T_pe, t + 1)
                if t >= 1:
                    act.wait_ge(logit_pe, t)
                for h in range(2):
                    nc.scalar.activation(h2T[:, 4 * h:4 * h + 4, :].rearrange("p k j -> p (k j)"), bank[4 + h][:],
                                         ACT.Copy).then_inc(h2T_ok, 1)
            act.wait_ge(logit_pe, NT)
            nc.scalar.activation(route[0], bank[6][:, 0:NT * E], ACT.Sigmoid).then_inc(score_ok, 1)

            def sel_copy(e):
                act.wait_ge(sel_pe, e + 1)
                for h in range(2):
                    nc.scalar.activation(xselT[:, 4 * h:4 * h + 4, :].rearrange("p k j -> p (k j)"), bank[5 + h][:],
                                         ACT.Copy).then_inc(sel_ok, 1)

            def silu(e):
                act.wait_ge(gu_pe, e + 1)
                nc.scalar.activation(silu_g, bank[0][:], ACT.Silu).then_inc(silu_ok, 1)

            def hid_copy(e):
                act.wait_ge(hidT_pe, e + 1)
                nc.scalar.activation(hidT.rearrange("p k j -> p (k j)"), bank[4][:], ACT.Copy).then_inc(hidT_ok, 1)

            sel_copy(0)
            for e in range(LOOP):
                silu(e)
                sel_copy(e + 1)
                hid_copy(e)
            with act.Fori(LOOP, E - 1) as e:
                silu(e)
                sel_copy(e + 1)
                hid_copy(e)
            silu(E - 1)
            hid_copy(E - 1)

            act.wait_ge(over_ok, 1)
            n_over = act.value_load(over_n[0:1, 0:1], min_val=0, max_val=MOST_OVER)
            with act.If(n_over > 0):
                with act.Fori(0, n_over) as o:
                    act.wait_ge(o_sel_pe, o + 1)
                    for h in range(2):
                        nc.scalar.activation(xselT[:, 4 * h:4 * h + 4, :].rearrange("p k j -> p (k j)"), bank[5 + h][:],
                                             ACT.Copy).then_inc(o_sel, 1)
                    act.wait_ge(o_gu, o + 1)
                    nc.scalar.activation(silu_g, bank[0][:], ACT.Silu).then_inc(o_silu, 1)
                    act.wait_ge(o_hidT_pe, o + 1)
                    nc.scalar.activation(hidT.rearrange("p k j -> p (k j)"), bank[4][:], ACT.Copy).then_inc(o_hidT, 1)

            act.wait_ge(h2_stored, 16 * NT)
            act.dma_start(final_bc, final_g.rearrange("(a d) -> a d", a=1).to_broadcast([P, D])).then_inc(final_in, 16)
            for t in range(NT):
                act.wait_ge(all_rows, t + 1)
                nc.scalar.activation(res[t], x_sb[:, t, :], ACT.Square, accum_out=stat[:, 0, t:t + 1]).then_inc(fin_sq, 1)
                act.wait_ge(fin_stat, t + 1)
                nc.scalar.activation(stat[:, 1, t:t + 1], stat[:, 3, t:t + 1], ACT.Sqrt).then_inc(fin_root, 1)

        @block.vector
        def _(dve):
            V = nc.vector
            count = [0]

            def link(ins):
                count[0] += 1
                ins.then_inc(order, 1)
                dve.wait_ge(order, count[0])

            def mean_square(cols, signal):
                V.tensor_scalar(stat[:, 3, cols], stat[:, 0, cols], 1.0 / D, EPS, ALU.mult, ALU.add).then_inc(signal, 1)

            def inverse_root(cols, n, signal):
                r, v, w = stat[:, 2, cols], stat[:, 3, cols], stat[:, 0, cols]
                link(V.reciprocal(r, stat[:, 1, cols]))
                link(V.tensor_tensor(w, r, r, ALU.mult))
                link(V.tensor_tensor(w, w, v, ALU.mult))
                link(V.tensor_scalar(w, w, -0.5, 1.5, ALU.mult, ALU.add))
                V.tensor_tensor(r, r, w, ALU.mult).then_inc(signal, 1)

            dve.wait_ge(prmT_pe, 1)
            V.tensor_copy(prmT[:], bank[7][:, 0:32]).then_inc(prmT_ok, 1)
            dve.wait_ge(cact_ok, 1)

            def ada(j, k):
                n = 8 * j + k
                if j < 2:
                    dve.wait_ge(ada1_in[n // 2], 16)
                else:
                    dve.wait_ge(ada2_in[(n - 16) // 4], 16)
                if k == 0:
                    dve.wait_ge(brow_in[j], 16)
                if n:
                    dve.wait_ge(ada_ok, n)
                V.scalar_tensor_tensor(out=acc[:, j % 2, :], in0=ring_k[ADA_SLOTS[j][k // 4]][:, k % 4, :],
                                       scalar=c_act[:, k:k + 1], in1=acc[:, j % 2, :],
                                       op0=ALU.mult, op1=ALU.add).then_inc(ada_ok, 1)

            for k in range(KD):
                ada(0, k)
            dve.wait_ge(sq_ok, NT)
            mean_square(slice(0, NT), ms_ok)
            dve.wait_ge(pads_ok, 3)
            V.reciprocal(icnt[:], icnt[:]).then_inc(icnt_ok, 1)
            for k in range(4):
                ada(1, k)
            dve.wait_ge(ms_ok, 1)
            dve.wait_ge(root_ok, 1)
            inverse_root(slice(0, NT), 1, rstd_ok)
            for k in range(4, KD):
                ada(1, k)
            dve.wait_ge(acc_used, 2)
            dve.wait_ge(prmT_ok, 1)
            V.tensor_copy(mod1[:, 0, :], bank[7][:, 0:KD]).then_inc(mod1_ok, 1)
            V.scalar_tensor_tensor(out=mod1[:, 1, :], in0=bank[7][:, KD:2 * KD], scalar=1.0, in1=prmT[:, KD:2 * KD],
                                   op0=ALU.add, op1=ALU.mult).then_inc(mod1_ok, 1)
            dve.wait_ge(mod1_ok, 2)
            dve.wait_ge(xT_ok, KD)
            for k in range(0, KD, 2):
                V.tensor_scalar(hT[:, k, :], hT[:, k, :], mod1[:, 1, k:k + 1], mod1[:, 0, k:k + 1],
                                ALU.mult, ALU.add).then_inc(hT_dve, 1)

            todo = [(j, k) for j in range(2, 6) for k in range(KD)]
            dve.wait_ge(icnt_ok, 1)
            for n, (m, i) in enumerate(tiles):
                if m == "v":
                    dve.wait_ge(act_ev, i + 1)
                    src, win = vpad, WINDOWS[i]
                    for s in range(i + 1):
                        step, to = 1 << s, (sum_a, sum_b)[s % 2]
                        lo = 2 * step - 1
                        link(V.tensor_tensor(to[:, lo:], src[:, lo:], src[:, lo - step:PAD + T - step], ALU.add))
                        src = to
                    o = yT[:, NC + i, :]
                    link(V.tensor_tensor(o[:, 0:win], src[:, PAD:PAD + win], icnt[:, 0:win], ALU.mult))
                    link(V.tensor_tensor(o[:, 0:win], o[:, 0:win], vpad[:, PAD:PAD + win], ALU.subtract))
                    V.scalar_tensor_tensor(out=o[:, win:], in0=src[:, PAD + win:], scalar=1.0 / win,
                                           in1=vpad[:, PAD + win:], op0=ALU.mult, op1=ALU.subtract).then_inc(pooled_ok, 1)
                if m == "h":
                    dve.wait_ge(proj_pe, n + 1)
                    dve.wait_ge(act_ev, NG + i + 1)
                    V.tensor_tensor(gpad[:, TAPS - 1:TAPS - 1 + T], bank[n % 4][:], sum_a[:, 0:T],
                                    ALU.mult).then_inc(dve_ev, 1)
                    dve.wait_ge(dve_ev, 2 * i + 1)
                    tap = lambda k: prmT[:, 2 * KD + k * NC + i:2 * KD + k * NC + i + 1]
                    link(V.tensor_scalar(sum_b[:, 0:T], gpad[:, 0:T], tap(0), None, ALU.mult))
                    for k in range(1, TAPS):
                        link(V.scalar_tensor_tensor(out=sum_b[:, 0:T], in0=gpad[:, k:k + T], scalar=tap(k),
                                                    in1=sum_b[:, 0:T], op0=ALU.mult, op1=ALU.add))
                if m == "B":
                    dve.wait_ge(proj_pe, n + 1)
                    V.tensor_tensor(yT[:, i, :], bank[n % 4][:], sum_b[:, 0:T], ALU.mult).then_inc(dve_ev, 1)
                if n >= ADA_FROM:
                    for j, k in todo[:ADA_PER]:
                        ada(j, k)
                    todo = todo[ADA_PER:]
                if REDUCE_AFTER.get(n) == 4:
                    dve.wait_ge(bc_pe, 3)
                    dve.wait_ge(norm2_in, 16)
                    for h in range(2):
                        part = scale2_bc[:, h * HALF:(h + 1) * HALF]
                        V.scalar_tensor_tensor(out=part, in0=bank[6 + h][:], scalar=1.0, in1=part,
                                               op0=ALU.add, op1=ALU.mult).then_inc(scale_ok, 1)
            for j, k in todo:
                ada(j, k)

            dve.wait_ge(filled, 32)
            dve.wait_ge(bc_ev, 4)
            dve.wait_ge(scale_ok, 2)
            for t in range(NT):
                dve.wait_ge(mix_pe, t + 1)
                for h in range(2):
                    cols = slice(h * HALF, (h + 1) * HALF)
                    link(V.tensor_tensor(h2[t][:, cols], bank[2 * (t % 2) + h][:], gate_bc[:, cols], ALU.mult))
                V.tensor_tensor(x_sb[:, t, :], x_sb[:, t, :], h2[t], ALU.add).then_inc(x2_ok, 1)
                one = slice(t, t + 1)
                dve.wait_ge(sq2_ok, t + 1)
                mean_square(one, ms2_ok)
                dve.wait_ge(ms2_ok, t + 1)
                dve.wait_ge(root2_ok, t + 1)
                inverse_root(one, t + 1, rstd2_ok)
                dve.wait_ge(xn2_ok, t + 1)
                link(V.tensor_tensor(h2[t], h2[t], scale2_bc[:], ALU.mult))
                V.tensor_tensor(h2[t], h2[t], shift2_bc[:], ALU.add).then_inc(h2_ok, 1)

            def tt(to, a, b, op):
                link(V.tensor_tensor(to, a, b, op))

            def by(ap, **k):
                return ap.rearrange("p (t g j) -> p t g j", t=NT, g=EG)

            def mid(ap):
                return ap.unsqueeze(2).to_broadcast([P, NT, EG, GRP])

            def last(ap):
                return ap.unsqueeze(3).to_broadcast([P, NT, EG, GRP])

            def rows4(i, lo=0):
                return route[i][:, lo:lo + NT * GRP].rearrange("p (t g) -> p t g", t=NT)

            four = lambda ap: ap.unsqueeze(2).to_broadcast([P, NT, GRP])
            tile4 = lambda i: route[i][:, 0:NT]
            desc4 = desc[:].unsqueeze(1).to_broadcast([P, NT, GRP])

            def first_max(vals, to, z):
                top = tile4(5)
                link(V.tensor_reduce(top, vals, AX_X, ALU.max))
                tt(z, vals, four(top), ALU.is_equal)
                tt(z, z, desc4, ALU.mult)
                link(V.tensor_reduce(top, z, AX_X, ALU.max))
                tt(to, z, four(top), ALU.is_equal)

            dve.wait_ge(score_ok, 1)
            dve.wait_ge(bias_in, 16)
            dve.wait_ge(const_ok, 9)
            s, sel = route[0], route[1]
            tt(sel.rearrange("p (t e) -> p t e", t=NT), s.rearrange("p (t e) -> p t e", t=NT),
               bias_bc[:].unsqueeze(1).to_broadcast([P, NT, E]), ALU.add)
            n2, n1 = NT * E // 2, NT * E // 4
            pairs = sel.rearrange("p (n two) -> p n two", two=2)
            tt(route[2][:, 0:n2], pairs[:, :, 0], pairs[:, :, 1], ALU.max)
            tt(route[3][:, 0:n2], pairs[:, :, 0], pairs[:, :, 1], ALU.min)
            hi = route[2][:, 0:n2].rearrange("p (n two) -> p n two", two=2)
            lo = route[3][:, 0:n2].rearrange("p (n two) -> p n two", two=2)
            tt(route[4][:, 0:n1], hi[:, :, 0], hi[:, :, 1], ALU.max)
            tt(route[4][:, n1:2 * n1], hi[:, :, 0], hi[:, :, 1], ALU.min)
            tt(route[4][:, 2 * n1:3 * n1], lo[:, :, 0], lo[:, :, 1], ALU.max)
            tt(route[4][:, n1:2 * n1], route[4][:, n1:2 * n1], route[4][:, 2 * n1:3 * n1], ALU.max)
            tt(route[4][:, 0:n1], route[4][:, 0:n1], route[4][:, n1:2 * n1], ALU.add)
            group = rows4(6)
            first_max(rows4(4), group, rows4(6, n1))
            tt(by(route[7]), by(sel), last(group), ALU.mult)
            tt(by(route[8]), by(s), last(group), ALU.mult)
            best, score = rows4(9), rows4(9, n1)
            link(V.tensor_reduce(best, by(route[7]).rearrange("p t g j -> p t j g"), AX_X, ALU.add))
            link(V.tensor_reduce(score, by(route[8]).rearrange("p t g j -> p t j g"), AX_X, ALU.add))
            one, two, z = rows4(10), rows4(10, n1), rows4(10, 2 * n1)
            first_max(best, one, z)
            link(V.scalar_tensor_tensor(out=best, in0=one, scalar=-BIG, in1=best, op0=ALU.mult, op1=ALU.add))
            first_max(best, two, z)
            low, high = rows4(11), rows4(11, n1)
            tt(z, one, two, ALU.add)
            tt(low, z, desc4, ALU.mult)
            link(V.tensor_reduce(tile4(5), low, AX_X, ALU.max))
            tt(low, low, four(tile4(5)), ALU.is_equal)
            tt(high, z, low, ALU.subtract)
            m_low, m_high, mask = route[12], route[13], route[14][:, 0:NT * E // 2].bitcast(BF16)
            tt(by(m_low), last(group), mid(low), ALU.mult)
            tt(by(m_high), last(group), mid(high), ALU.mult)
            V.tensor_tensor(mask, m_low, m_high, ALU.add).then_inc(mask_ok, 1)
            tt(low, low, score, ALU.mult)
            tt(high, high, score, ALU.mult)
            link(V.tensor_reduce(combine[:, 0, :], low, AX_X, ALU.add))
            link(V.tensor_reduce(combine[:, 1, :], high, AX_X, ALU.add))
            tt(tile4(5), combine[:, 0, :], combine[:, 1, :], ALU.add)
            link(V.reciprocal(tile4(5), tile4(5)))
            tt(combine[:, :, :], combine[:, :, :], tile4(5).unsqueeze(1).to_broadcast([P, 2, NT]), ALU.mult)

            dve.wait_ge(rank_pe, 1)
            rank, place = route[15], route[16]
            V.tensor_copy(route[15:17][0], bank[7][:, 0:NT * E]).then_inc(rank_ev, 1)
            counts = route[17][:, 0:E]
            V.tensor_copy(counts, bank[7][:, NT * E:(NT + 1) * E]).then_inc(rank_ev, 1)
            dve.wait_ge(rank_ev, 2)
            dve.wait_ge(mask_ok, 1)
            link(V.scalar_tensor_tensor(out=place, in0=rank, scalar=1.0, in1=mask, op0=ALU.add, op1=ALU.mult))
            link(V.tensor_scalar(place, place, -1.0, None, ALU.add))

            def token_numbers(b):
                for t in range(NT):
                    q = place[:, t * E + b * GRP:t * E + (b + 1) * GRP]
                    ins = V.tensor_tensor(onehot[:, t, b * GRP:(b + 1) * GRP, :],
                                          q.unsqueeze(2).to_broadcast([P, GRP, P]),
                                          iota_j[:].unsqueeze(1).to_broadcast([P, GRP, P]), ALU.is_equal)
                ins.then_inc(hot_ok, 1)

            def read_numbers(b):
                dve.wait_ge(idx_pe, b + 1)
                mine = slice(b * GRP, (b + 1) * GRP)
                V.tensor_copy(idx_main[:, mine], bank[7][:, mine]).then_inc(idx_ok, 1)

            token_numbers(0)
            token_numbers(1)
            read_numbers(0)
            token_numbers(2)
            read_numbers(1)
            token_numbers(3)
            read_numbers(2)
            read_numbers(3)

            beyond, shift, slot = route[17][:, E:2 * E], route[17][:, 2 * E:3 * E], route[18]
            link(V.tensor_scalar(beyond, counts, float(P), None, ALU.is_gt))
            for k in range(2, NT):
                link(V.scalar_tensor_tensor(out=beyond, in0=counts, scalar=float(k * P), in1=beyond,
                                            op0=ALU.is_gt, op1=ALU.add))
            link(V.tensor_tensor_scan(over_sum[:], ones[:, 0:E], beyond, 0.0, ALU.mult, ALU.add))
            tt(shift, over_sum[:], beyond, ALU.subtract)
            tt(shift, shift, iota_e[:], ALU.subtract)
            link(V.tensor_scalar(shift, shift, float(P), float(MAIN - P), ALU.mult, ALU.add))
            wide = lambda ap: ap.unsqueeze(1).to_broadcast([P, NT, E])
            te = lambda ap: ap.rearrange("p (t e) -> p t e", t=NT)
            link(V.scalar_tensor_tensor(out=te(slot), in0=te(rank), scalar=float(P), in1=wide(shift),
                                        op0=ALU.is_ge, op1=ALU.mult))
            tt(slot, slot, rank, ALU.add)
            link(V.tensor_scalar(route[19][:, 0:E], iota_e[:], float(P), None, ALU.mult))
            tt(te(slot), te(slot), wide(route[19][:, 0:E]), ALU.add)
            for i, m in enumerate((m_low, m_high)):
                tt(route[20], m, slot, ALU.mult)
                link(V.tensor_reduce(over_rel[:, i, :], te(route[20]), AX_X, ALU.add))
            V.tensor_copy(slot_u[:], over_rel[:]).then_inc(slots_ok, 1)
            dve.wait_ge(slots_ok, 1)
            link(V.tensor_scalar(over_rel[:], over_rel[:], float(-MAIN), None, ALU.add))
            link(V.memset(over_k[:], 0.0))
            V.tensor_copy(over_n[:, 0:1], over_sum[:, E - 1:E]).then_inc(over_ok, 1)

            def hidden(e):
                dve.wait_ge(silu_ok, e + 1)
                V.tensor_tensor(hid, bank[1][:], silu_g, ALU.mult).then_inc(hid_ok, 1)

            def rows(e, i, free):
                if free is not None:
                    dve.wait_ge(stored[i], free)
                dve.wait_ge(y_pe, e + 1)
                for h in range(2):
                    cols = slice(h * HALF, (h + 1) * HALF)
                    V.tensor_tensor(y_sb[i][:, cols], bank[2 + h][:], gate_bc[:, cols], ALU.mult).then_inc(y_ok, 1)

            dve.wait_ge(gate2_ok, 2)
            hidden(0)
            hidden(1)
            rows(0, 0, None)
            hidden(2)
            rows(1, 1, None)
            with dve.Fori(LOOP, E - 1, 2) as e:
                hidden(e)
                rows(e - 1, 0, (e - 1) * 8)
                hidden(e + 1)
                rows(e, 1, (e - 1) * 8)
            hidden(E - 1)
            rows(E - 2, 0, (E - 2) * 8)
            rows(E - 1, 1, (E - 2) * 8)

            STEPS = STEPS_OVER
            dve.wait_ge(over_ok, 1)
            n_over = dve.value_load(over_n[0:1, 0:1], min_val=0, max_val=MOST_OVER)
            for i in range(2):
                dve.wait_ge(stored[i], 16 * (E // 2))
            with dve.If(n_over > 0):
                with dve.Fori(0, n_over) as o:
                    step = [0]

                    def olink(ins):
                        step[0] += 1
                        ins.then_inc(o_order, 1)
                        dve.wait_ge(o_order, STEPS * o + step[0])

                    olink(V.tensor_scalar(over_cmp[:], over_sum[:], over_k[:, 0:1], None, ALU.is_le))
                    olink(V.tensor_reduce(over_e, over_cmp, AX_X, ALU.add))
                    V.tensor_copy(over_n[:, 1:2], over_e).then_inc(o_pick, 1)
                    for t in range(NT):
                        olink(V.tensor_scalar(over_hot[:, t, :], iota_j[:], over_rel[:, 0, t:t + 1], None, ALU.is_equal))
                        olink(V.scalar_tensor_tensor(out=over_hot[:, t, :], in0=iota_j[:], scalar=over_rel[:, 1, t:t + 1],
                                                     in1=over_hot[:, t, :], op0=ALU.is_equal, op1=ALU.add))
                    olink(V.tensor_scalar(over_rel[:], over_rel[:], float(-P), None, ALU.add))
                    olink(V.tensor_scalar(over_k[:], over_k[:], 1.0, None, ALU.add))
                    dve.wait_ge(o_idx_pe, o + 1)
                    V.tensor_copy(idx_over[:, 0:1], bank[7][:, 0:1]).then_inc(o_idx, 1)
                    dve.wait_ge(o_silu, o + 1)
                    V.tensor_tensor(hid, bank[1][:], silu_g, ALU.mult).then_inc(o_hid, 1)
                    dve.wait_ge(o_y_pe, o + 1)
                    for h in range(2):
                        cols = slice(h * HALF, (h + 1) * HALF)
                        V.tensor_tensor(y_sb[0][:, cols], bank[2 + h][:], gate_bc[:, cols], ALU.mult).then_inc(o_y, 1)
                    dve.wait_ge(o_stored, 16 * o + 16)
                    assert step[0] == STEPS

            def finish(t):
                one = slice(t, t + 1)
                dve.wait_ge(fin_sq, t + 1)
                mean_square(one, fin_stat)
                dve.wait_ge(fin_stat, t + 1)
                dve.wait_ge(fin_root, t + 1)
                inverse_root(one, t + 1, fin_rstd)
                dve.wait_ge(fin_rstd, t + 1)
                dve.wait_ge(final_in, 16)
                V.scalar_tensor_tensor(out=res[t], in0=x_sb[:, t, :], scalar=stat[:, 2, t:t + 1], in1=final_bc,
                                       op0=ALU.mult, op1=ALU.mult).then_inc(res_ok, 1)

            for t in range(NT):
                dve.wait_ge(tok_in[t], 32)
                link(V.scalar_tensor_tensor(out=x_sb[:, t, :], in0=ya[t], scalar=combine[:, 0, t:t + 1],
                                            in1=x_sb[:, t, :], op0=ALU.mult, op1=ALU.add))
                V.scalar_tensor_tensor(out=x_sb[:, t, :], in0=yb[t], scalar=combine[:, 1, t:t + 1],
                                       in1=x_sb[:, t, :], op0=ALU.mult, op1=ALU.add).then_inc(all_rows, 1)
                if t >= 1:
                    finish(t - 1)
            finish(NT - 1)

        @block.tensor
        def _(pe):
            mm = nc.tensor.matmul
            pe.wait_ge(const_ok, 1)
            pe.wait_ge(prm_in, 64)
            nc.tensor.transpose(bank[7][:, 0:32], prm[:, :], ident[0:32, 0:32]).then_inc(prmT_pe, 1)
            pe.wait_ge(xn_ok, NT)
            pe.wait_ge(prmT_ok, 1)
            for k in range(KD):
                for t in range(NT):
                    last = nc.tensor.transpose(bank[k][:, t * P:(t + 1) * P],
                                               yflat[:, t * D + k * P:t * D + (k + 1) * P], ident[:])
                last.then_inc(xT_pe, 1)
            pe.wait_ge(const_ok, 2)
            pe.wait_ge(xT_ok, KD)
            for j in range(2):
                pe.wait_ge(ada_ok, 8 * (j + 1))
                for k in range(KD):
                    last = mm(bank[7][:, j * KD + k:j * KD + k + 1], acc[:, j, k * P:(k + 1) * P], ones[:, 0:1],
                              start=True, stop=True)
                last.then_inc(acc_used, 1)

            def pool_map(g):
                pe.wait_ge(pooled_ok, g + 1)
                if g == 0:
                    pe.wait_ge(poolw_in, 16)
                if g >= 2:
                    pe.wait_ge(pool_ev, g - 1)
                mm(bank[4 + g % 2][:], pool_w_sb[:, g, :], yT[:, NC + g, :], start=True, stop=True).then_inc(pool_pe, 1)

            def spread(j, b, signal):
                pe.wait_ge(ada_ok, 8 * (j + 1))
                for h in range(2):
                    last = mm(bank[b + h][:], ones[:], acc[:, j % 2, h * HALF:(h + 1) * HALF], start=True, stop=True)
                last.then_inc(signal, 1)

            for n, (m, i) in enumerate(tiles):
                if i == 0:
                    pe.wait_ge(win_in[WORDER.index(m)], 16)
                if n >= 4:
                    pe.wait_ge(*freed[n - 4])
                for k in range(KD):
                    if n == 0:
                        pe.wait_ge(hT_act if k % 2 else hT_dve, k // 2 + 1)
                    last = mm(bank[n % 4][:], ring_w[WSLOT[m]][:, k, i * P:(i + 1) * P], hT[:, k, :],
                              start=k == 0, stop=k == KD - 1)
                last.then_inc(proj_pe, 1)
                if 1 <= n <= NG:
                    pool_map(n - 1)
                if n in REDUCE_AFTER:
                    j = REDUCE_AFTER[n]
                    if j > 2:
                        pe.wait_ge(bc_ev, 2 * (j - 2))
                    spread(j, 6, bc_pe)

            def logits(t):
                pe.wait_ge(h2_ok, t + 1)
                for k in range(KD):
                    last = nc.tensor.transpose(bank[4 + k // 4][:, (k % 4) * P:(k % 4 + 1) * P],
                                               h2[t][:, k * P:(k + 1) * P], ident[:])
                last.then_inc(h2T_pe, 1)
                pe.wait_ge(h2T_ok, 2 * t + 2)
                for k in range(KD):
                    last = mm(bank[6][:, t * E:(t + 1) * E], h2T[:, k, :], wr[:, k, :], start=k == 0, stop=k == KD - 1)
                last.then_inc(logit_pe, 1)

            pe.wait_ge(wout_in, 16)
            pe.wait_ge(dve_ev, 2 * NC)
            pe.wait_ge(pool_ev, NG)
            pe.wait_ge(wr_in, 16)
            for t in range(NT):
                if t >= 2:
                    pe.wait_ge(x2_ok, t - 1)
                for h in range(2):
                    for k in range(KD):
                        last = mm(bank[2 * (t % 2) + h][:], yT[:, k, t * P:(t + 1) * P],
                                  wout_sb[:, k, h * HALF:(h + 1) * HALF], start=k == 0, stop=k == KD - 1)
                last.then_inc(mix_pe, 1)
                if t == 0:
                    pe.wait_ge(scale_ok, 2)
                if t >= 1:
                    logits(t - 1)
            pe.wait_ge(x2_ok, NT - 1)
            spread(5, 0, gate2_pe)
            logits(NT - 1)

            pe.wait_ge(mask_ok, 1)
            pe.wait_ge(const_ok, 9)
            mask = route[14][:, 0:NT * E // 2].bitcast(BF16).rearrange("p (t e) -> p t e", t=NT)
            for t in range(NT + 1):
                for q in range(min(t + 1, NT)):
                    last = mm(bank[7][:, t * E:(t + 1) * E], before[:] if q == t else ones_h[:], mask[:, q, :],
                              start=q == 0, stop=q == min(t, NT - 1))
            last.then_inc(rank_pe, 1)

            def sel(e, i, value):
                pe.wait_ge(gathered[i], value)
                for k in range(KD):
                    last = nc.tensor.transpose(bank[5 + k // 4][:, (k % 4) * P:(k % 4 + 1) * P],
                                               xg[i][:, k * P:(k + 1) * P], ident[:])
                last.then_inc(sel_pe, 1)

            for b in range(E // GRP):
                pe.wait_ge(hot_ok, b + 1)
                pe.wait_ge(*((rank_ev, 2) if b == 0 else (idx_ok, b)))
                for e in range(b * GRP, (b + 1) * GRP):
                    for t in range(NT):
                        for i in range(2):
                            last = mm(bank[7][:, e:e + 1], onehot[:, t, e, :], tok_id[:, t, i:i + 1],
                                      start=t == 0 and i == 0, stop=t == NT - 1 and i == 1)
                last.then_inc(idx_pe, 1)

            def gate_up(waits, slots):
                for k in range(KD):
                    if waits and k % 4 == 0:
                        pe.wait_ge(*waits[k // 4])
                    for h in range(2):
                        last = mm(bank[h][:], xselT[:, k, :], ring_k[slots[k // 4]][:, k % 4, h * F:(h + 1) * F],
                                  start=k == 0, stop=k == KD - 1)
                    if k == 3 and waits:
                        last.then_inc(half_pe, 1)
                return last

            def down(slot):
                for h in range(2):
                    for k in range(KF):
                        last = mm(bank[2 + h][:], hidT[:, k, :], ring_k[slot][:, k, h * HALF:(h + 1) * HALF],
                                  start=k == 0, stop=k == KF - 1)
                return last

            def hidden(e):
                pe.wait_ge(hid_ok, e + 1)
                for k in range(KF):
                    last = nc.tensor.transpose(bank[4][:, k * P:(k + 1) * P], hid[:, k * P:(k + 1) * P], ident[:])
                last.then_inc(hidT_pe, 1)

            def down_rows(e, slot, value):
                pe.wait_ge(slot_in[slot], value)
                pe.wait_ge(hidT_ok, e + 1)
                down(slot).then_inc(y_pe, 1)

            def expert(e, odd):
                h16 = 8 * (e - 1) if odd else 8 * e
                pe.wait_ge(sel_ok, 2 * e + 2)
                if odd:
                    waits, slots, d_slot, d_value = [(slot_in[0], h16 + 16), (slot_in[1], h16 + 16)], (0, 1), 2, h16 + 16
                else:
                    waits, slots, d_slot, d_value = [(slot_in[3], h16), (slot_in[4], h16 + 16)], (3, 4), 5, h16 + 16
                gate_up(waits, slots).then_inc(gu_pe, 1)
                if not (isinstance(e, int) and e == E - 1):
                    sel(e + 1, 0 if odd else 1, h16 + 32 if odd else h16 + 16)
                if not (isinstance(e, int) and e == 1):
                    pe.wait_ge(y_ok, 2 * e - 2)
                down_rows(e - 1, d_slot, d_value)
                hidden(e)

            sel(0, 0, 16)
            pe.wait_ge(gate2_ok, 2)
            pe.wait_ge(sel_ok, 2)
            gate_up([(slot_in[4], 16), (slot_in[5], 16)], (4, 5)).then_inc(gu_pe, 1)
            sel(1, 1, 16)
            hidden(0)
            expert(1, True)
            expert(2, False)
            with pe.Fori(LOOP, E - 1, 2) as e:
                expert(e, True)
                expert(e + 1, False)
            expert(E - 1, True)
            pe.wait_ge(y_ok, 2 * E - 2)
            down_rows(E - 1, 5, 8 * (E + 2))

            pe.wait_ge(over_ok, 1)
            n_over = pe.value_load(over_n[0:1, 0:1], min_val=0, max_val=MOST_OVER)
            with pe.If(n_over > 0):
                with pe.Fori(0, n_over) as o:
                    pe.wait_ge(o_order, STEPS_OVER * o + 2 * NT + 2)
                    for t in range(NT):
                        for i in range(2):
                            last = mm(bank[7][:, 0:1], over_hot[:, t, :], tok_id[:, t, i:i + 1],
                                      start=t == 0 and i == 0, stop=t == NT - 1 and i == 1)
                    last.then_inc(o_idx_pe, 1)
                    pe.wait_ge(o_gathered, 16 * o + 16)
                    for k in range(KD):
                        last = nc.tensor.transpose(bank[5 + k // 4][:, (k % 4) * P:(k % 4 + 1) * P],
                                                   xg[0][:, k * P:(k + 1) * P], ident[:])
                    last.then_inc(o_sel_pe, 1)
                    pe.wait_ge(o_sel, 2 * o + 2)
                    pe.wait_ge(o_w, 48 * o + 48)
                    gate_up(None, (0, 1)).then_inc(o_gu, 1)
                    pe.wait_ge(o_hid, o + 1)
                    for k in range(KF):
                        last = nc.tensor.transpose(bank[4][:, k * P:(k + 1) * P], hid[:, k * P:(k + 1) * P], ident[:])
                    last.then_inc(o_hidT_pe, 1)
                    pe.wait_ge(o_hidT, o + 1)
                    down(2).then_inc(o_y_pe, 1)


_INS = ['x', 'c', 'w_in', 'conv_w', 'pool_w', 'pool_scale', 'w_out', 'norm1_g', 'norm2_g',
        'w_ada', 'b_ada', 'w_router', 'router_bias', 'w_gate_up', 'w_down', 'final_g']
_OUTS = [((1, 512, 1024), 'float32')]


def kernel(**inputs):
    import numpy as _np
    import concourse.bacc as _bacc
    from concourse import mybir as _mybir
    from concourse.bass_utils import run_bass_kernel_spmd as _run

    nc = _bacc.Bacc("TRN2", target_bir_lowering=False, num_devices=1)
    arrays, args = {}, []
    for name in _INS:
        a = _np.ascontiguousarray(inputs[name])
        arrays[f"in_{name}_dram"] = a
        args.append(nc.dram_tensor(f"in_{name}_dram", a.shape, _mybir.dt.from_np(a.dtype), kind="ExternalInput").ap())
    for i, (shape, dtype) in enumerate(_OUTS):
        dt = _mybir.dt.from_np(_np.dtype(dtype))
        args.append(nc.dram_tensor(f"out_{i}_dram", shape, dt, kind="ExternalOutput").ap())
    hybrid_block(nc, *args)
    r = _run(nc, [arrays], core_ids=[0])
    return r.results[0]["out_0_dram"]
```

```python
from contextlib import ExitStack

import concourse.bass as bass
from concourse import mybir

F32 = mybir.dt.float32
F32R = mybir.dt.float32r
BF16 = mybir.dt.bfloat16
U32 = mybir.dt.uint32
I32 = mybir.dt.int32
ALU = mybir.AluOpType
ACT = mybir.ActivationFunctionType
AX_X = mybir.AxisListType.X

P = 128
EPS = 1e-6
BIG = 1e30


def hybrid_block(nc, x, c, w_in, conv_w, pool_w, pool_scale, w_out, norm1_g, norm2_g,
                 w_ada, b_ada, w_router, router_bias, w_gate_up, w_down, final_g, out):
    T, D = x.shape[1], x.shape[2]
    NT, KD = T // P, D // P
    CW = conv_w.shape[2]
    NC = CW // P
    NG = pool_w.shape[1]
    WINDOWS = [2 << g for g in range(NG)]
    PAD = WINDOWS[-1]
    TAPS = conv_w.shape[1]
    E = w_router.shape[1]
    GRP = 4
    EG = E // GRP
    F = w_down.shape[2]
    KF = F // P
    HALF = D // 2
    PIECE = 4 * D
    MAIN = E * P
    MOST_OVER = 2 * T // P - 1

    ctx = ExitStack()
    with ctx:
        def sb(name, shape, dt=F32):
            return ctx.enter_context(nc.sbuf_tensor(name, shape, dt))

        def sem(name):
            return ctx.enter_context(nc.semaphore(name))

        bank = [ctx.enter_context(nc.psum_tensor(f"bank{i}", [P, HALF], F32)) for i in range(8)]

        ring = sb("ring", [P, 6, PIECE])
        x_sb = sb("x_sb", [P, NT, D])
        high = sb("high", [P, KD * T + D], F32R)
        low = sb("low", [P, KD * T + D], F32R)
        work = sb("work", [P, 3 * F])
        yT = sb("yT", [P, KD, T])
        acc = sb("acc", [P, 2, D])
        gate_bc = sb("gate_bc", [P, D])
        scale2_bc = sb("scale2_bc", [P, D])
        shift2_bc = sb("shift2_bc", [P, D])
        mixbuf = sb("mixbuf", [P, 4 * (PAD + T)])
        ident = sb("ident", [P, P])
        ones = sb("ones", [P, P])
        before = sb("before", [P, P], BF16)
        ones_h = sb("ones_h", [P, P], BF16)
        prm = sb("prm", [32, P])
        prmT = sb("prmT", [P, 32])
        c_act = sb("c_act", [P, KD])
        mod1 = sb("mod1", [P, 2, KD])
        icnt = sb("icnt", [P, PAD])
        stat = sb("stat", [P, 4, NT])
        wr = sb("wr", [P, KD, E])
        bias_bc = sb("bias_bc", [P, E])
        iota_j = sb("iota_j", [P, P], BF16)
        tok_id = sb("tok_id", [P, NT, 2], BF16)
        iota_e = sb("iota_e", [P, E])
        desc = sb("desc", [P, GRP])
        idx_main = sb("idx_main", [P, E], U32)
        idx_over = sb("idx_over", [P, 1], U32)
        slot_u = sb("slot_u", [P, 2, NT], U32)
        over_n = sb("over_n", [P, 2], I32)

        vpad, sum_a, sum_b, gpad = (mixbuf[:, i * (PAD + T):(i + 1) * (PAD + T)] for i in range(4))
        route = [mixbuf[:, i * NT * E:(i + 1) * NT * E] for i in range(22)]
        tail = mixbuf[:, 22 * NT * E:]
        combine = tail[:, 0:2 * NT].rearrange("p (i t) -> p i t", i=2)
        over_rel = tail[:, 2 * NT:4 * NT].rearrange("p (i t) -> p i t", i=2)
        over_sum, over_cmp = tail[:, E:2 * E], tail[:, 2 * E:3 * E]
        over_k, over_e = tail[:, 3 * E:3 * E + 1], tail[:, 3 * E + 1:3 * E + 2]

        yflat = yT[:, :, :].rearrange("p k t -> p (k t)")
        onehot = yflat[:, 0:T * E // 2].bitcast(BF16).rearrange("p (t e j) -> p t e j", t=NT, e=E)
        over_selT = yflat[:, 0:D].rearrange("p (k j) -> p k j", k=KD)
        over_hot = yflat[:, D:D + NT * P // 2].bitcast(BF16).rearrange("p (t j) -> p t j", t=NT)
        final_bc = yflat[:, 3 * D:4 * D]
        xg = [scale2_bc[:, :], shift2_bc[:, :]]
        y_sb = [acc[:, 0, :], acc[:, 1, :]]
        silu_g, hid = work[:, 0:F], work[:, F:2 * F]
        hidT = work[:, 2 * F:3 * F].rearrange("p (k j) -> p k j", k=KF)
        pool_w_sb = work[:, 0:NG * P].rearrange("p (g d) -> p g d", g=NG)
        h2 = [mixbuf[:, (t % 2) * D:(t % 2 + 1) * D] for t in range(NT)]
        h2T = acc[:, 0, :].rearrange("p (k j) -> p k j", k=KD)
        hT = [part[:, 0:KD * T].rearrange("p (k t) -> p k t", k=KD) for part in (high, low)]
        wsplit = [part[:, KD * T:].rearrange("p (b k m) -> p b k m", b=2, k=4) for part in (high, low)]
        wchunk = [part[:, 0:KD * T].rearrange("p (b n) -> p b n", b=4) for part in (high, low)]
        xselT = [part[:, KD * T:].rearrange("p (k j) -> p k j", k=KD) for part in (high, low)]
        as_f32 = lambda ap: ap.bitcast(F32)
        ring_k = [ring[:, s, :].rearrange("p (k n) -> p k n", k=4) for s in range(6)]
        ring_w = [ring[:, s, :].rearrange("p (k n) -> p k n", k=KD) for s in range(6)]
        wout_k = [ring_k[2 + k // 4][:, k % 4, :] for k in range(KD)]
        ring_flat = ring[:, :, :].rearrange("p s n -> p (s n)")
        ya = [ring_flat[:, t * D:(t + 1) * D] for t in range(NT)]
        yb = [ring_flat[:, (NT + t) * D:(NT + t + 1) * D] for t in range(NT)]
        res = [ring_flat[:, (2 * NT + t) * D:(2 * NT + t + 1) * D] for t in range(NT)]

        h2_dram = nc.dram_tensor("h2_rows", [T, D], F32)
        y_dram = nc.dram_tensor("y_rows", [MAIN + MOST_OVER * P, D], F32)

        prm_in, wr_in, bias_in, poolw_in, norm2_in, final_in = (
            sem(n) for n in ("prm_in", "wr_in", "bias_in", "poolw_in", "norm2_in", "final_in"))
        ada1_in = [sem(f"ada1_in{i}") for i in range(8)]
        x_in = sem("x_in")
        win_in = [sem(f"win_in{i}") for i in range(4)]
        ada2_in = [sem(f"ada2_in{i}") for i in range(8)]
        wout_in = [sem(f"wout_in{i}") for i in range(2)]
        slot_in = [sem(f"slot_in{i}") for i in range(6)]
        brow_in = [sem(f"brow_in{i}") for i in range(6)]
        const_ok, acc_zero, pads_ok, pool_order = (sem(n) for n in ("const_ok", "acc_zero", "pads_ok", "pool_order"))
        prmT_pe, prmT_ok, cact_ok, ada_ok, acc_used = (
            sem(n) for n in ("prmT_pe", "prmT_ok", "cact_ok", "ada_ok", "acc_used"))
        sq_ok, ms_ok, root_ok, rstd_ok, xn_ok, xT_pe, xT_ok = (
            sem(n) for n in ("sq_ok", "ms_ok", "root_ok", "rstd_ok", "xn_ok", "xT_pe", "xT_ok"))
        mod1_ok, proj_half, act_ev, dve_ev = (
            sem(n) for n in ("mod1_ok", "proj_half", "act_ev", "dve_ev"))
        pooled_ok, pool_pe, pool_ev, conv_ok, bc_pe, bc_ev, shift_ok, scale_ok = (
            sem(n) for n in ("pooled_ok", "pool_pe", "pool_ev", "conv_ok", "bc_pe", "bc_ev", "shift_ok", "scale_ok"))
        mix_pe, x2_ok, sq2_ok, ms2_ok, root2_ok, rstd2_ok, xn2_ok, h2_ok = (
            sem(n) for n in ("mix_pe", "x2_ok", "sq2_ok", "ms2_ok", "root2_ok", "rstd2_ok", "xn2_ok", "h2_ok"))
        h2T_pe, h2T_ok, logit_pe, score_ok = (
            sem(n) for n in ("h2T_pe", "h2T_ok", "logit_pe", "score_ok"))
        h2_stored = [sem(f"h2_stored{t}") for t in range(NT)]
        hT_full, hT_high, hT_low, w_high, w_low = (
            sem(n) for n in ("hT_full", "hT_high", "hT_low", "w_high", "w_low"))
        gu_high, gu_low, chunk_pe, sel_low = (sem(n) for n in ("gu_high", "gu_low", "chunk_pe", "sel_low"))
        mask_ok, rank_pe, rank_ev, hot_ok, idx_pe, idx_ok, slots_ok, over_ok = (
            sem(n) for n in ("mask_ok", "rank_pe", "rank_ev", "hot_ok", "idx_pe", "idx_ok", "slots_ok", "over_ok"))
        gate2_pe, gate2_ok = sem("gate2_pe"), sem("gate2_ok")
        icnt_ok, filled = sem("icnt_ok"), sem("filled")
        order = sem("vector_order")
        gathered = [sem("gathered0"), sem("gathered1")]
        stored = [sem("stored0"), sem("stored1")]
        sel_pe, sel_ok, silu_ok, hid_ok, hidT_pe, hidT_ok, y_pe, y_ok = (
            sem(n) for n in ("sel_pe", "sel_ok", "silu_ok", "hid_ok", "hidT_pe",
                             "hidT_ok", "y_pe", "y_ok"))
        o_pick, o_idx_pe, o_idx, o_sel_pe, o_sel, o_w, o_gu, o_silu, o_hid, o_hidT_pe, o_hidT, o_y_pe, o_y = (
            sem("over_" + n) for n in ("pick", "idx_pe", "idx", "sel_pe", "sel", "w", "gu", "silu",
                                       "hid", "hidT_pe", "hidT", "y_pe", "y"))
        o_gathered, o_stored, o_order, o_seen = (sem("over_" + n) for n in ("gathered", "stored", "order", "seen"))
        all_rows, fin_rstd, fin_stat, fin_sq, fin_root, res_ok, out_in = (
            sem(n) for n in ("all_rows", "fin_rstd", "fin_stat", "fin_sq", "fin_root", "res_ok", "out_in"))
        tok_in = [sem(f"tok_in{t}") for t in range(NT)]

        tiles = [("v", g) for g in range(NG)] + [(m, i) for i in range(NC) for m in ("C", "h", "B")]
        GROUP = {"B": 0, "C": 1, "h": 2, "v": 3}
        WSLOT = {"v": 4, "C": 5, "h": 0, "B": 1}
        WORDER = ["v", "C", "h", "B"]
        n_act = n_dve = 0
        freed = []
        for m, _ in tiles:
            if m in ("v", "C"):
                n_act += 1
                freed.append((act_ev, n_act))
            else:
                n_dve += 1
                freed.append((dve_ev, n_dve))
        ADA_SLOTS = [(0, 1), (2, 3), (2, 3), (4, 2), (3, 4), (0, 1)]
        REDUCE_AFTER = {9: 2, 11: 3, 14: 4}
        ADA_FROM, ADA_PER = 5, 3
        BEFORE_MIX = 24

        def w_half(n, half):
            m, i = tiles[n]
            return ring_w[WSLOT[m]][:, 4 * half:4 * half + 4, i * P:(i + 1) * P]

        block = ctx.enter_context(nc.Block())
        LOOP = 3
        STEPS_OVER = 2 * NT + 4

        def gate_up_place(e, odd):
            if isinstance(e, int) and e == 0:
                return (4, 5), [(slot_in[4], 16), (slot_in[5], 16)]
            if odd:
                return (0, 1), [(slot_in[0], 8 * e + 8), (slot_in[1], 8 * e + 8)]
            return (3, 4), [(slot_in[3], 8 * e), (slot_in[4], 8 * e + 16)]

        @block.sync
        def _(sp):
            def ada(j, half, to, signals, ks):
                src = w_ada[0, half * 4 * P:(half * 4 + 4) * P, j * D:(j + 1) * D].rearrange("(k p) n -> p k n", p=P)
                for q in range(0, 4, ks):
                    sp.dma_start(ring_k[to][:, q:q + ks, :], src[:, q:q + ks, :]).then_inc(signals[q // ks], 16)

            ada(0, 0, 0, ada1_in[0:2], 2)
            sp.dma_start(x_sb[:, :, :], x[0].rearrange("(t p) d -> p t d", p=P)).then_inc(x_in, 16)
            ada(0, 1, 1, ada1_in[2:4], 2)
            ada(1, 0, 2, ada1_in[4:6], 2)
            ada(1, 1, 3, ada1_in[6:8], 2)
            for n, m in enumerate(WORDER):
                if m == "h":
                    sp.wait_ge(ada_ok, 4)
                if m == "B":
                    sp.wait_ge(ada_ok, 8)
                g = GROUP[m]
                sp.dma_start(ring_w[WSLOT[m]][:, :, :],
                             w_in[0, :, g * CW:(g + 1) * CW].rearrange("(k p) n -> p k n", p=P)).then_inc(win_in[n], 16)
            for j in range(2, 5):
                for half in range(2):
                    n = 2 * (j - 2) + half
                    if n == 2:
                        sp.wait_ge(w_low, 2 * NG)
                    else:
                        sp.wait_ge(ada_ok, {0: 12, 1: 16}.get(n, 4 * (n + 2)))
                    ada(j, half, ADA_SLOTS[j][half], [ada2_in[n]], 4)
            for half in range(2):
                sp.wait_ge(ada_ok, (32, 36)[half])
                sp.dma_start(ring_k[2 + half][:, :, :], w_out[0, half * 4 * P:(half + 1) * 4 * P, :]
                             .rearrange("(k p) n -> p k n", p=P)).then_inc(wout_in[half], 16)
            for lo in range(0, MOST_OVER, NT):
                n = min(NT, MOST_OVER - lo)
                sp.dma_start(y_dram[MAIN + lo * P:MAIN + (lo + n) * P, :].rearrange("(t p) d -> p t d", p=P),
                             x_sb[:, 0:n, :]).then_inc(filled, 16)

            def gate_up(e, half, to):
                src = w_gate_up[0, bass.ds(e, 1), half * 4 * P:(half * 4 + 4) * P, :]
                sp.dma_start(ring_k[to][:, :, :], src.rearrange("a (k p) n -> p (a k) n", p=P)).then_inc(slot_in[to], 16)

            def down(e, to):
                src = w_down[0, bass.ds(e, 1)]
                sp.dma_start(ring_k[to][:, :, :], src.rearrange("a (k p) n -> p (a k) n", p=P)).then_inc(slot_in[to], 16)

            sp.wait_ge(ada_ok, 40)
            gate_up(0, 0, 4)
            sp.wait_ge(w_low, 2 * len(tiles))
            gate_up(0, 1, 5)
            ada(5, 0, 0, [ada2_in[6]], 4)
            ada(5, 1, 1, [ada2_in[7]], 4)
            sp.wait_ge(ada_ok, 44)
            gate_up(1, 0, 0)
            sp.wait_ge(ada_ok, 48)
            gate_up(1, 1, 1)
            sp.wait_ge(mix_pe, NT)
            down(0, 2)
            gate_up(2, 0, 3)
            sp.wait_ge(gu_low, 4)
            gate_up(2, 1, 4)
            sp.wait_ge(gu_low, 8)
            down(1, 5)

            def refill(e, s):
                sp.wait_ge(gu_low, 8 * e - 12)
                gate_up(e, 0, s)
                sp.wait_ge(gu_low, 8 * e - 8)
                gate_up(e, 1, s + 1)
                sp.wait_ge(y_pe, e - 2)
                down(e - 1, s + 2)

            with sp.Fori(LOOP, E - 1, 2) as e:
                refill(e, 0)
                refill(e + 1, 3)
            refill(E - 1, 0)
            sp.wait_ge(y_pe, E - 2)
            down(E - 1, 5)

            sp.wait_ge(over_ok, 1)
            n_over = sp.value_load(over_n[0:1, 0:1], min_val=0, max_val=MOST_OVER)
            sp.wait_ge(y_pe, E)
            with sp.If(n_over > 0):
                with sp.Fori(0, n_over) as o:
                    sp.wait_ge(o_pick, o + 1)
                    sp.sem_inc(o_seen, 1)
                    ex = sp.value_load(over_n[0:1, 1:2], min_val=0, max_val=E - 1)
                    for half in range(2):
                        src = w_gate_up[0, bass.ds(ex, 1), half * 4 * P:(half * 4 + 4) * P, :]
                        sp.dma_start(ring_k[half][:, :, :], src.rearrange("a (k p) n -> p (a k) n", p=P)).then_inc(o_w, 16)
                    sp.dma_start(ring_k[2][:, :, :],
                                 w_down[0, bass.ds(ex, 1)].rearrange("a (k p) n -> p (a k) n", p=P)).then_inc(o_w, 16)

            for t in range(NT):
                sp.wait_ge(res_ok, t + 1)
                sp.dma_start(out[0, t * P:(t + 1) * P, :], res[t]).then_inc(out_in, 16)
            sp.wait_ge(out_in, 16 * NT)

        @block.gpsimd
        def _(pool):
            nc.gpsimd.memset(ident[:], 0.0).then_inc(pool_order, 1)
            nc.gpsimd.memset(acc[:, 0, :], 0.0).then_inc(acc_zero, 1)
            pool.wait_ge(pool_order, 1)
            nc.gpsimd.affine_select(out=ident[:], in_=ident[:], compare_op=ALU.not_equal, fill=1.0, base=0,
                                    pattern=[[-1, P]], channel_multiplier=1).then_inc(const_ok, 1)
            nc.gpsimd.memset(acc[:, 1, :], 0.0).then_inc(acc_zero, 1)
            for j in range(2):
                pool.wait_ge(acc_zero, j + 1)
                pool.dma_start(acc[0:1, j, :], b_ada[:, j * D:(j + 1) * D]).then_inc(brow_in[j], 16)
            nc.gpsimd.memset(ones[:], 1.0).then_inc(const_ok, 1)
            nc.gpsimd.memset(vpad[:, 0:PAD], 0.0).then_inc(pads_ok, 1)
            nc.gpsimd.memset(gpad[:, 0:TAPS - 1], 0.0).then_inc(pads_ok, 1)
            iota = lambda to, pattern, base, step: nc.gpsimd.iota(
                to, pattern=pattern, base=base, channel_multiplier=step, allow_small_or_imprecise_dtypes=True)
            iota(icnt[:], [[1, PAD]], 1, 0).then_inc(pads_ok, 1)
            nc.gpsimd.memset(before[:], 1.0).then_inc(pool_order, 1)
            pool.wait_ge(pool_order, 2)
            nc.gpsimd.affine_select(out=before[:], in_=before[:], compare_op=ALU.is_gt, fill=0.0, base=0,
                                    pattern=[[1, P]], channel_multiplier=-1).then_inc(const_ok, 1)
            nc.gpsimd.memset(ones_h[:], 1.0).then_inc(const_ok, 1)
            iota(iota_j[:], [[1, P]], 0, 0).then_inc(const_ok, 1)
            iota(iota_e[:], [[1, E]], 0, 0).then_inc(const_ok, 1)
            iota(desc[:], [[-1, GRP]], GRP, 0).then_inc(const_ok, 1)
            iota(tok_id[:, :, 0], [[0, NT]], 0, 1).then_inc(const_ok, 1)
            iota(tok_id[:, :, 1], [[P, NT]], 0, 0).then_inc(const_ok, 1)
            for j in range(2, 6):
                pool.wait_ge(*((acc_used, j - 1) if j < 4 else (bc_pe, j - 3)))
                nc.gpsimd.memset(acc[:, j % 2, :], 0.0).then_inc(acc_zero, 1)
                pool.wait_ge(acc_zero, j + 1)
                pool.dma_start(acc[0:1, j % 2, :], b_ada[:, j * D:(j + 1) * D]).then_inc(brow_in[j], 16)
            for t in range(NT):
                pool.wait_ge(h2_ok, t + 1)
                pool.dma_start(h2_dram[t * P:(t + 1) * P, :], h2[t]).then_inc(h2_stored[t], 16)
            for t in range(NT):
                pool.wait_ge(h2_stored[t], 16)

            def gather(idx, to, signal):
                pool.indirect_dma_start(out=to, out_offset=None, in_=h2_dram[:, :],
                                        in_offset=bass.IndirectOffsetOnAxis(ap=idx, axis=0)).then_inc(signal, 16)

            def store(e):
                pool.wait_ge(y_ok, 2 * (e + 1))
                pool.dma_start(y_dram[e * P:(e + 1) * P, :], y_sb[e % 2]).then_inc(stored[e % 2], 16)

            for e in range(2):
                pool.wait_ge(idx_ok, 1)
                gather(idx_main[:, e:e + 1], xg[e], gathered[e])
            for e in range(E):
                if e + 2 < E:
                    if (e + 2) % GRP == 0:
                        pool.wait_ge(idx_ok, (e + 2) // GRP + 1)
                    pool.wait_ge(sel_pe, e + 1)
                    gather(idx_main[:, e + 2:e + 3], xg[e % 2], gathered[e % 2])
                if e >= 2:
                    store(e - 2)
            for e in range(E - 2, E):
                store(e)

            pool.wait_ge(over_ok, 1)
            n_over = pool.value_load(over_n[0:1, 0:1], min_val=0, max_val=MOST_OVER)
            for i in range(2):
                pool.wait_ge(stored[i], 16 * (E // 2))
            with pool.If(n_over > 0):
                with pool.Fori(0, n_over) as o:
                    pool.wait_ge(o_idx, o + 1)
                    pool.sem_inc(o_seen, 1)
                    gather(idx_over[:, 0:1], xg[0], o_gathered)
                    pool.wait_ge(o_y, 2 * o + 2)
                    pool.dma_start(y_dram[bass.ds(MAIN + o * P, P), :], y_sb[0]).then_inc(o_stored, 16)
                    pool.wait_ge(o_stored, 16 * o + 16)
            pool.wait_ge(slots_ok, 1)
            for t in range(NT):
                for i, to in enumerate((ya[t], yb[t])):
                    pool.indirect_dma_start(out=to, out_offset=None, in_=y_dram[:, :],
                                            in_offset=bass.IndirectOffsetOnAxis(ap=slot_u[:, i, t:t + 1], axis=0)
                                            ).then_inc(tok_in[t], 16)

        @block.scalar
        def _(act):
            rows = 2 * KD
            act.dma_start(prm[0:KD, :], c.rearrange("b (k p) -> (b k) p", p=P)).then_inc(prm_in, 16)
            act.dma_start(prm[KD:rows, :], norm1_g.rearrange("b (k p) -> (b k) p", p=P)).then_inc(prm_in, 16)
            act.dma_start(prm[rows:rows + TAPS * NC, :],
                          conv_w.rearrange("l k (i p) -> (l k i) p", p=P)).then_inc(prm_in, 16)
            act.dma_start(prm[rows + TAPS * NC:32, :], pool_scale.rearrange("l (i p) -> (l i) p", p=P)).then_inc(prm_in, 16)
            act.dma_start(pool_w_sb, pool_w[0].rearrange("g c d -> c g d")).then_inc(poolw_in, 16)
            act.dma_start(wr[:, :, :], w_router.rearrange("(k p) e -> p k e", p=P)).then_inc(wr_in, 16)
            act.dma_start(bias_bc[:, :], router_bias.rearrange("(a e) -> a e", a=1).to_broadcast([P, E])).then_inc(bias_in, 16)
            act.dma_start(scale2_bc[:, :], norm2_g.to_broadcast([P, D])).then_inc(norm2_in, 16)

            act.wait_ge(prmT_ok, 1)
            nc.scalar.activation(c_act[:], prmT[:, 0:KD], ACT.Silu).then_inc(cact_ok, 1)
            act.wait_ge(x_in, 16)
            for t in range(NT):
                nc.scalar.activation(yflat[:, t * D:(t + 1) * D], x_sb[:, t, :], ACT.Square,
                                     accum_out=stat[:, 0, t:t + 1]).then_inc(sq_ok, 1)
            act.wait_ge(ms_ok, 1)
            nc.scalar.activation(stat[:, 1, :], stat[:, 3, :], ACT.Sqrt).then_inc(root_ok, 1)
            act.wait_ge(rstd_ok, 1)
            act.wait_ge(sq_ok, NT)
            for t in range(NT):
                nc.scalar.activation(yflat[:, t * D:(t + 1) * D], x_sb[:, t, :], ACT.Copy,
                                     scale=stat[:, 2, t:t + 1]).then_inc(xn_ok, 1)
            act.wait_ge(xT_pe, KD)
            for k in range(KD):
                nc.scalar.activation(yT[:, k, :], bank[k][:], ACT.Copy).then_inc(xT_ok, 1)

            def split_half(n, half):
                m, i = tiles[n]
                if i == 0 and half == 0:
                    act.wait_ge(win_in[WORDER.index(m)], 16)
                b = 2 * n + half
                if b >= 2:
                    act.wait_ge(proj_half, b - 1)
                nc.scalar.activation(wsplit[0][:, b % 2], w_half(n, half), ACT.Copy).then_inc(w_high, 1)

            for k in range(KD):
                act.wait_ge(hT_full, k + 1)
                nc.scalar.activation(hT[0][:, k, :], yT[:, k, :], ACT.Copy).then_inc(hT_high, 1)
                if k == 1:
                    split_half(0, 0)

            def evacuate(n):
                m, i = tiles[n]
                if m == "v":
                    act.wait_ge(proj_half, 2 * n + 2)
                    if i == 0:
                        act.wait_ge(pads_ok, 3)
                    else:
                        act.wait_ge(pooled_ok, i)
                    nc.scalar.activation(vpad[:, PAD:], bank[n % 4][:], ACT.Copy).then_inc(act_ev, 1)
                if m == "C":
                    if i == 0:
                        act.wait_ge(pooled_ok, NG)
                    else:
                        act.wait_ge(dve_ev, 2 * i - 1)
                    act.wait_ge(proj_half, 2 * n + 2)
                    nc.scalar.activation(sum_a[:, 0:T], bank[n % 4][:], ACT.Copy).then_inc(act_ev, 1)

            def after(n):
                evacuate(n)
                if 2 <= n <= NG + 1:
                    g = n - 2
                    act.wait_ge(pool_pe, g + 1)
                    o = rows + TAPS * NC + g
                    nc.scalar.activation(yT[:, NC + g, :], bank[4 + g % 2][:], ACT.Copy,
                                         scale=prmT[:, o:o + 1]).then_inc(pool_ev, 1)
                j = REDUCE_AFTER.get(n)
                if j in (2, 3):
                    act.wait_ge(bc_pe, j - 1)
                    for h in range(2):
                        nc.scalar.activation((gate_bc if j == 2 else shift2_bc)[:, h * HALF:(h + 1) * HALF],
                                             bank[6 + h][:], ACT.Copy).then_inc(bc_ev, 1)

            for n, (m, i) in enumerate(tiles):
                if n:
                    split_half(n, 0)
                split_half(n, 1)
                if n:
                    after(n - 1)
            after(len(tiles) - 1)

            for t in range(NT):
                act.wait_ge(x2_ok, t + 1)
                nc.scalar.activation(h2[t], x_sb[:, t, :], ACT.Square, accum_out=stat[:, 0, t:t + 1]).then_inc(sq2_ok, 1)
                act.wait_ge(ms2_ok, t + 1)
                nc.scalar.activation(stat[:, 1, t:t + 1], stat[:, 3, t:t + 1], ACT.Sqrt).then_inc(root2_ok, 1)
                act.wait_ge(rstd2_ok, t + 1)
                act.wait_ge(sq2_ok, t + 1)
                nc.scalar.activation(h2[t], x_sb[:, t, :], ACT.Copy, scale=stat[:, 2, t:t + 1]).then_inc(xn2_ok, 1)
                if t == NT - 1:
                    act.wait_ge(gate2_pe, 1)
                    for h in range(2):
                        nc.scalar.activation(gate_bc[:, h * HALF:(h + 1) * HALF], bank[h][:], ACT.Copy).then_inc(gate2_ok, 1)
                act.wait_ge(h2T_pe, t + 1)
                if t >= 1:
                    act.wait_ge(logit_pe, t)
                for h in range(2):
                    nc.scalar.activation(h2T[:, 4 * h:4 * h + 4, :].rearrange("p k j -> p (k j)"), bank[4 + h][:],
                                         ACT.Copy).then_inc(h2T_ok, 1)
            act.wait_ge(logit_pe, NT)
            for t in range(NT):
                act.wait_ge(h2_stored[t], 16)
            nc.scalar.activation(route[0], bank[6][:, 0:NT * E], ACT.Sigmoid).then_inc(score_ok, 1)

            def split(e, chunks, slots, waits=None):
                for k in chunks:
                    if k % 4 == 0:
                        act.wait_ge(*waits[k // 4])
                    if not (isinstance(e, int) and e == 0 and k < 4):
                        act.wait_ge(chunk_pe, 8 * e + k - 3)
                    nc.scalar.activation(wchunk[0][:, k % 4], ring_k[slots[k // 4]][:, k % 4, :],
                                         ACT.Copy).then_inc(gu_high, 1)

            def sel_copy(e):
                act.wait_ge(sel_pe, e + 1)
                for h in range(2):
                    nc.scalar.activation(xselT[0][:, 4 * h:4 * h + 4, :].rearrange("p k j -> p (k j)"), bank[5 + h][:],
                                         ACT.Copy).then_inc(sel_ok, 1)

            def silu(e):
                act.wait_ge(chunk_pe, 8 * e + 8)
                nc.scalar.activation(silu_g, bank[0][:], ACT.Silu).then_inc(silu_ok, 1)

            def hid_copy(e):
                act.wait_ge(hidT_pe, e + 1)
                nc.scalar.activation(hidT.rearrange("p k j -> p (k j)"), bank[4][:], ACT.Copy).then_inc(hidT_ok, 1)

            def expert(e, odd, last=False):
                split(e, range(4, KD), *gate_up_place(e, odd))
                silu(e)
                if not last:
                    sel_copy(e + 1)
                    split(e + 1, range(4), *gate_up_place(e + 1, not odd))
                hid_copy(e)

            act.wait_ge(proj_half, 2 * len(tiles))
            split(0, range(4), *gate_up_place(0, False))
            sel_copy(0)
            for e in range(LOOP):
                expert(e, e % 2 == 1)
            with act.Fori(LOOP, E - 1, 2) as e:
                expert(e, True)
                expert(e + 1, False)
            expert(E - 1, True, last=True)

            act.wait_ge(over_ok, 1)
            n_over = act.value_load(over_n[0:1, 0:1], min_val=0, max_val=MOST_OVER)
            with act.If(n_over > 0):
                with act.Fori(0, n_over) as o:
                    act.wait_ge(o_sel_pe, o + 1)
                    for h in range(2):
                        nc.scalar.activation(over_selT[:, 4 * h:4 * h + 4, :].rearrange("p k j -> p (k j)"),
                                             bank[5 + h][:], ACT.Copy).then_inc(o_sel, 1)
                    act.wait_ge(o_gu, o + 1)
                    nc.scalar.activation(silu_g, bank[0][:], ACT.Silu).then_inc(o_silu, 1)
                    act.wait_ge(o_hidT_pe, o + 1)
                    nc.scalar.activation(hidT.rearrange("p k j -> p (k j)"), bank[4][:], ACT.Copy).then_inc(o_hidT, 1)

            act.wait_ge(idx_ok, E // GRP)
            act.dma_start(final_bc, final_g.rearrange("(a d) -> a d", a=1).to_broadcast([P, D])).then_inc(final_in, 16)
            for t in range(NT):
                act.wait_ge(all_rows, t + 1)
                nc.scalar.activation(res[t], x_sb[:, t, :], ACT.Square, accum_out=stat[:, 0, t:t + 1]).then_inc(fin_sq, 1)
                act.wait_ge(fin_stat, t + 1)
                nc.scalar.activation(stat[:, 1, t:t + 1], stat[:, 3, t:t + 1], ACT.Sqrt).then_inc(fin_root, 1)

        @block.vector
        def _(dve):
            V = nc.vector
            count = [0]

            def link(ins):
                count[0] += 1
                ins.then_inc(order, 1)
                dve.wait_ge(order, count[0])

            def mean_square(cols, signal):
                V.tensor_scalar(stat[:, 3, cols], stat[:, 0, cols], 1.0 / D, EPS, ALU.mult, ALU.add).then_inc(signal, 1)

            def inverse_root(cols, n, signal):
                r, v, w = stat[:, 2, cols], stat[:, 3, cols], stat[:, 0, cols]
                link(V.reciprocal(r, stat[:, 1, cols]))
                link(V.tensor_tensor(w, r, r, ALU.mult))
                link(V.tensor_tensor(w, w, v, ALU.mult))
                link(V.tensor_scalar(w, w, -0.5, 1.5, ALU.mult, ALU.add))
                V.tensor_tensor(r, r, w, ALU.mult).then_inc(signal, 1)

            dve.wait_ge(prmT_pe, 1)
            V.tensor_copy(prmT[:], bank[7][:, 0:32]).then_inc(prmT_ok, 1)
            dve.wait_ge(cact_ok, 1)

            def ada(j, k):
                n = 8 * j + k
                if j < 2:
                    dve.wait_ge(ada1_in[n // 2], 16)
                else:
                    dve.wait_ge(ada2_in[(n - 16) // 4], 16)
                if k == 0:
                    dve.wait_ge(brow_in[j], 16)
                if n:
                    dve.wait_ge(ada_ok, n)
                V.scalar_tensor_tensor(out=acc[:, j % 2, :], in0=ring_k[ADA_SLOTS[j][k // 4]][:, k % 4, :],
                                       scalar=c_act[:, k:k + 1], in1=acc[:, j % 2, :],
                                       op0=ALU.mult, op1=ALU.add).then_inc(ada_ok, 1)

            for k in range(KD):
                ada(0, k)
            dve.wait_ge(sq_ok, NT)
            mean_square(slice(0, NT), ms_ok)
            dve.wait_ge(pads_ok, 3)
            V.reciprocal(icnt[:], icnt[:]).then_inc(icnt_ok, 1)
            for k in range(4):
                ada(1, k)
            dve.wait_ge(ms_ok, 1)
            dve.wait_ge(root_ok, 1)
            inverse_root(slice(0, NT), 1, rstd_ok)
            for k in range(4, KD):
                ada(1, k)
            dve.wait_ge(acc_used, 2)
            dve.wait_ge(prmT_ok, 1)
            V.tensor_copy(mod1[:, 0, :], bank[7][:, 0:KD]).then_inc(mod1_ok, 1)
            V.scalar_tensor_tensor(out=mod1[:, 1, :], in0=bank[7][:, KD:2 * KD], scalar=1.0, in1=prmT[:, KD:2 * KD],
                                   op0=ALU.add, op1=ALU.mult).then_inc(mod1_ok, 1)
            dve.wait_ge(mod1_ok, 2)

            def norm_low(k):
                dve.wait_ge(hT_high, k + 1)
                V.tensor_tensor(hT[1][:, k, :], yT[:, k, :], as_f32(hT[0][:, k, :]), ALU.subtract).then_inc(hT_low, 1)

            def w_low_half(n, half):
                b = 2 * n + half
                dve.wait_ge(w_high, b + 1)
                V.tensor_tensor(wsplit[1][:, b % 2], w_half(n, half), as_f32(wsplit[0][:, b % 2]),
                                ALU.subtract).then_inc(w_low, 1)

            for k in range(KD):
                dve.wait_ge(xT_ok, k + 1)
                V.tensor_scalar(yT[:, k, :], yT[:, k, :], mod1[:, 1, k:k + 1], mod1[:, 0, k:k + 1],
                                ALU.mult, ALU.add).then_inc(hT_full, 1)
                if k:
                    norm_low(k - 1)
                if k == 2:
                    w_low_half(0, 0)
            norm_low(KD - 1)

            todo = [(j, k) for j in range(2, 6) for k in range(KD)]
            dve.wait_ge(icnt_ok, 1)

            def after(n):
                m, i = tiles[n]
                if m == "v":
                    dve.wait_ge(act_ev, i + 1)
                    src, win = vpad, WINDOWS[i]
                    for s in range(i + 1):
                        step, to = 1 << s, (sum_a, sum_b)[s % 2]
                        lo = 2 * step - 1
                        link(V.tensor_tensor(to[:, lo:], src[:, lo:], src[:, lo - step:PAD + T - step], ALU.add))
                        src = to
                    o = yT[:, NC + i, :]
                    link(V.tensor_tensor(o[:, 0:win], src[:, PAD:PAD + win], icnt[:, 0:win], ALU.mult))
                    link(V.tensor_tensor(o[:, 0:win], o[:, 0:win], vpad[:, PAD:PAD + win], ALU.subtract))
                    V.scalar_tensor_tensor(out=o[:, win:], in0=src[:, PAD + win:], scalar=1.0 / win,
                                           in1=vpad[:, PAD + win:], op0=ALU.mult, op1=ALU.subtract).then_inc(pooled_ok, 1)
                if m == "h":
                    dve.wait_ge(proj_half, 2 * n + 2)
                    dve.wait_ge(act_ev, NG + i + 1)
                    V.tensor_tensor(gpad[:, TAPS - 1:TAPS - 1 + T], bank[n % 4][:], sum_a[:, 0:T],
                                    ALU.mult).then_inc(dve_ev, 1)
                    dve.wait_ge(dve_ev, 2 * i + 1)
                    tap = lambda k: prmT[:, 2 * KD + k * NC + i:2 * KD + k * NC + i + 1]
                    link(V.tensor_scalar(sum_b[:, 0:T], gpad[:, 0:T], tap(0), None, ALU.mult))
                    for k in range(1, TAPS):
                        link(V.scalar_tensor_tensor(out=sum_b[:, 0:T], in0=gpad[:, k:k + T], scalar=tap(k),
                                                    in1=sum_b[:, 0:T], op0=ALU.mult, op1=ALU.add))
                if m == "B":
                    dve.wait_ge(proj_half, 2 * n + 2)
                    V.tensor_tensor(yT[:, i, :], bank[n % 4][:], sum_b[:, 0:T], ALU.mult).then_inc(dve_ev, 1)
                if REDUCE_AFTER.get(n) == 4:
                    dve.wait_ge(bc_pe, 3)
                    dve.wait_ge(norm2_in, 16)
                    for h in range(2):
                        part = scale2_bc[:, h * HALF:(h + 1) * HALF]
                        V.scalar_tensor_tensor(out=part, in0=bank[6 + h][:], scalar=1.0, in1=part,
                                               op0=ALU.add, op1=ALU.mult).then_inc(scale_ok, 1)

            for n in range(len(tiles)):
                if n:
                    w_low_half(n, 0)
                w_low_half(n, 1)
                if n:
                    after(n - 1)
                if n >= ADA_FROM:
                    for j, k in todo[:min(ADA_PER, len(todo) - (48 - 16 - BEFORE_MIX))]:
                        ada(j, k)
                    todo = todo[min(ADA_PER, len(todo) - (48 - 16 - BEFORE_MIX)):]
            after(len(tiles) - 1)

            dve.wait_ge(filled, 32)
            dve.wait_ge(bc_ev, 4)
            dve.wait_ge(scale_ok, 2)
            for t in range(NT):
                if t >= 2:
                    dve.wait_ge(h2T_pe, t - 1)
                    dve.wait_ge(h2_stored[t - 2], 16)
                dve.wait_ge(mix_pe, t + 1)
                for h in range(2):
                    cols = slice(h * HALF, (h + 1) * HALF)
                    link(V.tensor_tensor(h2[t][:, cols], bank[2 * (t % 2) + h][:], gate_bc[:, cols], ALU.mult))
                V.tensor_tensor(x_sb[:, t, :], x_sb[:, t, :], h2[t], ALU.add).then_inc(x2_ok, 1)
                one = slice(t, t + 1)
                dve.wait_ge(sq2_ok, t + 1)
                mean_square(one, ms2_ok)
                dve.wait_ge(ms2_ok, t + 1)
                dve.wait_ge(root2_ok, t + 1)
                inverse_root(one, t + 1, rstd2_ok)
                dve.wait_ge(xn2_ok, t + 1)
                link(V.tensor_tensor(h2[t], h2[t], scale2_bc[:], ALU.mult))
                V.tensor_tensor(h2[t], h2[t], shift2_bc[:], ALU.add).then_inc(h2_ok, 1)
                if t < NT - 1:
                    for j, k in todo[:3]:
                        ada(j, k)
                    todo = todo[3:]

            def tt(to, a, b, op):
                link(V.tensor_tensor(to, a, b, op))

            def by(ap, **k):
                return ap.rearrange("p (t g j) -> p t g j", t=NT, g=EG)

            def mid(ap):
                return ap.unsqueeze(2).to_broadcast([P, NT, EG, GRP])

            def last(ap):
                return ap.unsqueeze(3).to_broadcast([P, NT, EG, GRP])

            def rows4(i, lo=0):
                return route[i][:, lo:lo + NT * GRP].rearrange("p (t g) -> p t g", t=NT)

            four = lambda ap: ap.unsqueeze(2).to_broadcast([P, NT, GRP])
            tile4 = lambda i: route[i][:, 0:NT]
            desc4 = desc[:].unsqueeze(1).to_broadcast([P, NT, GRP])

            def first_max(vals, to, z):
                top = tile4(5)
                link(V.tensor_reduce(top, vals, AX_X, ALU.max))
                tt(z, vals, four(top), ALU.is_equal)
                tt(z, z, desc4, ALU.mult)
                link(V.tensor_reduce(top, z, AX_X, ALU.max))
                tt(to, z, four(top), ALU.is_equal)

            dve.wait_ge(score_ok, 1)
            dve.wait_ge(bias_in, 16)
            dve.wait_ge(const_ok, 9)
            s, sel = route[0], route[1]
            tt(sel.rearrange("p (t e) -> p t e", t=NT), s.rearrange("p (t e) -> p t e", t=NT),
               bias_bc[:].unsqueeze(1).to_broadcast([P, NT, E]), ALU.add)
            n2, n1 = NT * E // 2, NT * E // 4
            pairs = sel.rearrange("p (n two) -> p n two", two=2)
            tt(route[2][:, 0:n2], pairs[:, :, 0], pairs[:, :, 1], ALU.max)
            tt(route[3][:, 0:n2], pairs[:, :, 0], pairs[:, :, 1], ALU.min)
            hi = route[2][:, 0:n2].rearrange("p (n two) -> p n two", two=2)
            lo = route[3][:, 0:n2].rearrange("p (n two) -> p n two", two=2)
            tt(route[4][:, 0:n1], hi[:, :, 0], hi[:, :, 1], ALU.max)
            tt(route[4][:, n1:2 * n1], hi[:, :, 0], hi[:, :, 1], ALU.min)
            tt(route[4][:, 2 * n1:3 * n1], lo[:, :, 0], lo[:, :, 1], ALU.max)
            tt(route[4][:, n1:2 * n1], route[4][:, n1:2 * n1], route[4][:, 2 * n1:3 * n1], ALU.max)
            tt(route[4][:, 0:n1], route[4][:, 0:n1], route[4][:, n1:2 * n1], ALU.add)
            group = rows4(6)
            first_max(rows4(4), group, rows4(6, n1))
            tt(by(route[7]), by(sel), last(group), ALU.mult)
            tt(by(route[8]), by(s), last(group), ALU.mult)
            best, score = rows4(9), rows4(9, n1)
            link(V.tensor_reduce(best, by(route[7]).rearrange("p t g j -> p t j g"), AX_X, ALU.add))
            link(V.tensor_reduce(score, by(route[8]).rearrange("p t g j -> p t j g"), AX_X, ALU.add))
            one, two, z = rows4(10), rows4(10, n1), rows4(10, 2 * n1)
            first_max(best, one, z)
            link(V.scalar_tensor_tensor(out=best, in0=one, scalar=-BIG, in1=best, op0=ALU.mult, op1=ALU.add))
            first_max(best, two, z)
            low, high = rows4(11), rows4(11, n1)
            tt(z, one, two, ALU.add)
            tt(low, z, desc4, ALU.mult)
            link(V.tensor_reduce(tile4(5), low, AX_X, ALU.max))
            tt(low, low, four(tile4(5)), ALU.is_equal)
            tt(high, z, low, ALU.subtract)
            m_low, m_high, mask = route[12], route[13], route[14][:, 0:NT * E // 2].bitcast(BF16)
            tt(by(m_low), last(group), mid(low), ALU.mult)
            tt(by(m_high), last(group), mid(high), ALU.mult)
            V.tensor_tensor(mask, m_low, m_high, ALU.add).then_inc(mask_ok, 1)
            tt(low, low, score, ALU.mult)
            tt(high, high, score, ALU.mult)
            link(V.tensor_reduce(combine[:, 0, :], low, AX_X, ALU.add))
            link(V.tensor_reduce(combine[:, 1, :], high, AX_X, ALU.add))
            tt(tile4(5), combine[:, 0, :], combine[:, 1, :], ALU.add)
            link(V.reciprocal(tile4(5), tile4(5)))
            tt(combine[:, :, :], combine[:, :, :], tile4(5).unsqueeze(1).to_broadcast([P, 2, NT]), ALU.mult)

            dve.wait_ge(rank_pe, 1)
            rank, place = route[15], route[16]
            V.tensor_copy(route[15:17][0], bank[7][:, 0:NT * E]).then_inc(rank_ev, 1)
            counts = route[17][:, 0:E]
            V.tensor_copy(counts, bank[7][:, NT * E:(NT + 1) * E]).then_inc(rank_ev, 1)
            dve.wait_ge(rank_ev, 2)
            dve.wait_ge(mask_ok, 1)
            link(V.scalar_tensor_tensor(out=place, in0=rank, scalar=1.0, in1=mask, op0=ALU.add, op1=ALU.mult))
            link(V.tensor_scalar(place, place, -1.0, None, ALU.add))

            def token_numbers(b):
                for t in range(NT):
                    q = place[:, t * E + b * GRP:t * E + (b + 1) * GRP]
                    ins = V.tensor_tensor(onehot[:, t, b * GRP:(b + 1) * GRP, :],
                                          q.unsqueeze(2).to_broadcast([P, GRP, P]),
                                          iota_j[:].unsqueeze(1).to_broadcast([P, GRP, P]), ALU.is_equal)
                ins.then_inc(hot_ok, 1)

            def read_numbers(b):
                dve.wait_ge(idx_pe, b + 1)
                mine = slice(b * GRP, (b + 1) * GRP)
                V.tensor_copy(idx_main[:, mine], bank[7][:, mine]).then_inc(idx_ok, 1)

            token_numbers(0)
            token_numbers(1)
            read_numbers(0)
            dve.wait_ge(proj_half, 2 * len(tiles))
            for k in range(4):
                dve.wait_ge(gu_high, k + 1)
                V.tensor_tensor(wchunk[1][:, k], ring_k[4][:, k, :], as_f32(wchunk[0][:, k]),
                                ALU.subtract).then_inc(gu_low, 1)
            token_numbers(2)
            read_numbers(1)
            token_numbers(3)
            read_numbers(2)
            read_numbers(3)

            beyond, shift, slot = route[17][:, E:2 * E], route[17][:, 2 * E:3 * E], route[18]
            link(V.tensor_scalar(beyond, counts, float(P), None, ALU.is_gt))
            for k in range(2, NT):
                link(V.scalar_tensor_tensor(out=beyond, in0=counts, scalar=float(k * P), in1=beyond,
                                            op0=ALU.is_gt, op1=ALU.add))
            link(V.tensor_tensor_scan(over_sum[:], ones[:, 0:E], beyond, 0.0, ALU.mult, ALU.add))
            tt(shift, over_sum[:], beyond, ALU.subtract)
            tt(shift, shift, iota_e[:], ALU.subtract)
            link(V.tensor_scalar(shift, shift, float(P), float(MAIN - P), ALU.mult, ALU.add))
            wide = lambda ap: ap.unsqueeze(1).to_broadcast([P, NT, E])
            te = lambda ap: ap.rearrange("p (t e) -> p t e", t=NT)
            link(V.scalar_tensor_tensor(out=te(slot), in0=te(rank), scalar=float(P), in1=wide(shift),
                                        op0=ALU.is_ge, op1=ALU.mult))
            tt(slot, slot, rank, ALU.add)
            link(V.tensor_scalar(route[19][:, 0:E], iota_e[:], float(P), None, ALU.mult))
            tt(te(slot), te(slot), wide(route[19][:, 0:E]), ALU.add)
            for i, m in enumerate((m_low, m_high)):
                tt(route[20], m, slot, ALU.mult)
                link(V.tensor_reduce(over_rel[:, i, :], te(route[20]), AX_X, ALU.add))
            V.tensor_copy(slot_u[:], over_rel[:]).then_inc(slots_ok, 1)
            dve.wait_ge(slots_ok, 1)
            link(V.tensor_scalar(over_rel[:], over_rel[:], float(-MAIN), None, ALU.add))
            link(V.memset(over_k[:], 0.0))
            V.tensor_copy(over_n[:, 0:1], over_sum[:, E - 1:E]).then_inc(over_ok, 1)

            def split_low(e, chunks, slots, waits=None):
                for k in chunks:
                    dve.wait_ge(gu_high, 8 * e + k + 1)
                    V.tensor_tensor(wchunk[1][:, k % 4], ring_k[slots[k // 4]][:, k % 4, :],
                                    as_f32(wchunk[0][:, k % 4]), ALU.subtract).then_inc(gu_low, 1)

            def tokens_low(e):
                for h in range(2):
                    dve.wait_ge(sel_ok, 2 * e + h + 1)
                    cols = slice(4 * h, 4 * h + 4)
                    V.tensor_tensor(xselT[1][:, cols, :].rearrange("p k j -> p (k j)"), bank[5 + h][:],
                                    as_f32(xselT[0][:, cols, :].rearrange("p k j -> p (k j)")),
                                    ALU.subtract).then_inc(sel_low, 1)

            def hidden(e):
                dve.wait_ge(silu_ok, e + 1)
                V.tensor_tensor(hid, bank[1][:], silu_g, ALU.mult).then_inc(hid_ok, 1)

            def rows(e, i, free):
                if free is not None:
                    dve.wait_ge(stored[i], free)
                dve.wait_ge(y_pe, e + 1)
                for h in range(2):
                    cols = slice(h * HALF, (h + 1) * HALF)
                    V.tensor_tensor(y_sb[i][:, cols], bank[2 + h][:], gate_bc[:, cols], ALU.mult).then_inc(y_ok, 1)

            dve.wait_ge(gate2_ok, 2)
            tokens_low(0)

            def expert(e, odd, free, last=False):
                split_low(e, range(4, KD), *gate_up_place(e, odd))
                hidden(e)
                if not last:
                    tokens_low(e + 1)
                    split_low(e + 1, range(4), *gate_up_place(e + 1, not odd))
                if not (isinstance(e, int) and e == 0):
                    rows(e - 1, 0 if odd else 1, free)

            expert(0, False, None)
            expert(1, True, None)
            expert(2, False, None)
            with dve.Fori(LOOP, E - 1, 2) as e:
                expert(e, True, (e - 1) * 8)
                expert(e + 1, False, (e - 1) * 8)
            expert(E - 1, True, (E - 2) * 8, last=True)
            rows(E - 1, 1, (E - 2) * 8)

            STEPS = STEPS_OVER
            dve.wait_ge(over_ok, 1)
            n_over = dve.value_load(over_n[0:1, 0:1], min_val=0, max_val=MOST_OVER)
            for i in range(2):
                dve.wait_ge(stored[i], 16 * (E // 2))
            with dve.If(n_over > 0):
                with dve.Fori(0, n_over) as o:
                    step = [0]

                    def olink(ins):
                        step[0] += 1
                        ins.then_inc(o_order, 1)
                        dve.wait_ge(o_order, STEPS * o + step[0])

                    olink(V.tensor_scalar(over_cmp[:], over_sum[:], over_k[:, 0:1], None, ALU.is_le))
                    olink(V.tensor_reduce(over_e, over_cmp, AX_X, ALU.add))
                    V.tensor_copy(over_n[:, 1:2], over_e).then_inc(o_pick, 1)
                    for t in range(NT):
                        olink(V.tensor_scalar(over_hot[:, t, :], iota_j[:], over_rel[:, 0, t:t + 1], None, ALU.is_equal))
                        olink(V.scalar_tensor_tensor(out=over_hot[:, t, :], in0=iota_j[:], scalar=over_rel[:, 1, t:t + 1],
                                                     in1=over_hot[:, t, :], op0=ALU.is_equal, op1=ALU.add))
                    olink(V.tensor_scalar(over_rel[:], over_rel[:], float(-P), None, ALU.add))
                    olink(V.tensor_scalar(over_k[:], over_k[:], 1.0, None, ALU.add))
                    dve.wait_ge(o_idx_pe, o + 1)
                    V.tensor_copy(idx_over[:, 0:1], bank[7][:, 0:1]).then_inc(o_idx, 1)
                    dve.wait_ge(o_silu, o + 1)
                    V.tensor_tensor(hid, bank[1][:], silu_g, ALU.mult).then_inc(o_hid, 1)
                    dve.wait_ge(o_y_pe, o + 1)
                    for h in range(2):
                        cols = slice(h * HALF, (h + 1) * HALF)
                        V.tensor_tensor(y_sb[0][:, cols], bank[2 + h][:], gate_bc[:, cols], ALU.mult).then_inc(o_y, 1)
                    dve.wait_ge(o_stored, 16 * o + 16)
                    assert step[0] == STEPS

            def finish(t):
                one = slice(t, t + 1)
                dve.wait_ge(fin_sq, t + 1)
                mean_square(one, fin_stat)
                dve.wait_ge(fin_stat, t + 1)
                dve.wait_ge(fin_root, t + 1)
                inverse_root(one, t + 1, fin_rstd)
                dve.wait_ge(fin_rstd, t + 1)
                dve.wait_ge(final_in, 16)
                V.scalar_tensor_tensor(out=res[t], in0=x_sb[:, t, :], scalar=stat[:, 2, t:t + 1], in1=final_bc,
                                       op0=ALU.mult, op1=ALU.mult).then_inc(res_ok, 1)

            for t in range(NT):
                dve.wait_ge(tok_in[t], 32)
                link(V.scalar_tensor_tensor(out=x_sb[:, t, :], in0=ya[t], scalar=combine[:, 0, t:t + 1],
                                            in1=x_sb[:, t, :], op0=ALU.mult, op1=ALU.add))
                V.scalar_tensor_tensor(out=x_sb[:, t, :], in0=yb[t], scalar=combine[:, 1, t:t + 1],
                                       in1=x_sb[:, t, :], op0=ALU.mult, op1=ALU.add).then_inc(all_rows, 1)
                if t >= 1:
                    finish(t - 1)
            finish(NT - 1)

        @block.tensor
        def _(pe):
            mm = nc.tensor.matmul
            pe.wait_ge(const_ok, 1)
            pe.wait_ge(prm_in, 64)
            nc.tensor.transpose(bank[7][:, 0:32], prm[:, :], ident[0:32, 0:32]).then_inc(prmT_pe, 1)
            pe.wait_ge(xn_ok, NT)
            pe.wait_ge(prmT_ok, 1)
            for k in range(KD):
                for t in range(NT):
                    last = nc.tensor.transpose(bank[k][:, t * P:(t + 1) * P],
                                               yflat[:, t * D + k * P:t * D + (k + 1) * P], ident[:])
                last.then_inc(xT_pe, 1)
            pe.wait_ge(const_ok, 2)
            pe.wait_ge(xT_ok, KD)
            for j in range(2):
                pe.wait_ge(ada_ok, 8 * (j + 1))
                for k in range(KD):
                    last = mm(bank[7][:, j * KD + k:j * KD + k + 1], acc[:, j, k * P:(k + 1) * P], ones[:, 0:1],
                              start=True, stop=True)
                last.then_inc(acc_used, 1)

            def pool_map(g):
                pe.wait_ge(pooled_ok, g + 1)
                if g == 0:
                    pe.wait_ge(poolw_in, 16)
                if g >= 2:
                    pe.wait_ge(pool_ev, g - 1)
                mm(bank[4 + g % 2][:], pool_w_sb[:, g, :], yT[:, NC + g, :], start=True, stop=True).then_inc(pool_pe, 1)

            def spread(j, b, signal):
                pe.wait_ge(ada_ok, 8 * (j + 1))
                for h in range(2):
                    last = mm(bank[b + h][:], ones[:], acc[:, j % 2, h * HALF:(h + 1) * HALF], start=True, stop=True)
                last.then_inc(signal, 1)

            for n in range(len(tiles)):
                if n >= 4:
                    pe.wait_ge(*freed[n - 4])
                for k in range(KD):
                    if k % 4 == 0:
                        b = 2 * n + k // 4
                        pe.wait_ge(w_low, b + 1)
                    if n == 0:
                        pe.wait_ge(hT_low, k + 1)
                    for q, (w, h) in enumerate(((0, 0), (0, 1), (1, 0))):
                        last = mm(bank[n % 4][:], wsplit[w][:, b % 2, k % 4, :], hT[h][:, k, :],
                                  start=k == 0 and q == 0, stop=k == KD - 1 and q == 2)
                    if k % 4 == 3:
                        last.then_inc(proj_half, 1)
                if 1 <= n <= NG:
                    pool_map(n - 1)
                if n in REDUCE_AFTER:
                    j = REDUCE_AFTER[n]
                    if j > 2:
                        pe.wait_ge(bc_ev, 2 * (j - 2))
                    spread(j, 6, bc_pe)

            def logits(t):
                pe.wait_ge(h2_ok, t + 1)
                for k in range(KD):
                    last = nc.tensor.transpose(bank[4 + k // 4][:, (k % 4) * P:(k % 4 + 1) * P],
                                               h2[t][:, k * P:(k + 1) * P], ident[:])
                last.then_inc(h2T_pe, 1)
                pe.wait_ge(h2T_ok, 2 * t + 2)
                for k in range(KD):
                    last = mm(bank[6][:, t * E:(t + 1) * E], h2T[:, k, :], wr[:, k, :], start=k == 0, stop=k == KD - 1)
                last.then_inc(logit_pe, 1)

            for half in range(2):
                pe.wait_ge(wout_in[half], 16)
            pe.wait_ge(dve_ev, 2 * NC)
            pe.wait_ge(pool_ev, NG)
            pe.wait_ge(wr_in, 16)
            for t in range(NT):
                if t >= 2:
                    pe.wait_ge(x2_ok, t - 1)
                for h in range(2):
                    for k in range(KD):
                        last = mm(bank[2 * (t % 2) + h][:], yT[:, k, t * P:(t + 1) * P],
                                  wout_k[k][:, h * HALF:(h + 1) * HALF], start=k == 0, stop=k == KD - 1)
                last.then_inc(mix_pe, 1)
                if t == 0:
                    pe.wait_ge(scale_ok, 2)
                if t >= 1:
                    logits(t - 1)
            pe.wait_ge(x2_ok, NT - 1)
            spread(5, 0, gate2_pe)
            logits(NT - 1)

            pe.wait_ge(mask_ok, 1)
            pe.wait_ge(const_ok, 9)
            mask = route[14][:, 0:NT * E // 2].bitcast(BF16).rearrange("p (t e) -> p t e", t=NT)
            for t in range(NT + 1):
                for q in range(min(t + 1, NT)):
                    last = mm(bank[7][:, t * E:(t + 1) * E], before[:] if q == t else ones_h[:], mask[:, q, :],
                              start=q == 0, stop=q == min(t, NT - 1))
            last.then_inc(rank_pe, 1)

            def sel(e, i, value):
                pe.wait_ge(gathered[i], value)
                for k in range(KD):
                    last = nc.tensor.transpose(bank[5 + k // 4][:, (k % 4) * P:(k % 4 + 1) * P],
                                               xg[i][:, k * P:(k + 1) * P], ident[:])
                last.then_inc(sel_pe, 1)

            for b in range(E // GRP):
                pe.wait_ge(hot_ok, b + 1)
                pe.wait_ge(*((rank_ev, 2) if b == 0 else (idx_ok, b)))
                for e in range(b * GRP, (b + 1) * GRP):
                    for t in range(NT):
                        for i in range(2):
                            last = mm(bank[7][:, e:e + 1], onehot[:, t, e, :], tok_id[:, t, i:i + 1],
                                      start=t == 0 and i == 0, stop=t == NT - 1 and i == 1)
                last.then_inc(idx_pe, 1)

            def gate_up(e):
                for k in range(KD):
                    pe.wait_ge(gu_low, 8 * e + k + 1)
                    for q, (a, w) in enumerate(((0, 0), (0, 1), (1, 0))):
                        for h in range(2):
                            last = mm(bank[h][:], xselT[a][:, k, :], wchunk[w][:, k % 4, h * F:(h + 1) * F],
                                      start=k == 0 and q == 0, stop=k == KD - 1 and q == 2)
                    last.then_inc(chunk_pe, 1)

            def down(slot):
                for h in range(2):
                    for k in range(KF):
                        last = mm(bank[2 + h][:], hidT[:, k, :], ring_k[slot][:, k, h * HALF:(h + 1) * HALF],
                                  start=k == 0, stop=k == KF - 1)
                return last

            def hidden(e):
                pe.wait_ge(hid_ok, e + 1)
                for k in range(KF):
                    last = nc.tensor.transpose(bank[4][:, k * P:(k + 1) * P], hid[:, k * P:(k + 1) * P], ident[:])
                last.then_inc(hidT_pe, 1)

            def down_rows(e, slot, value):
                pe.wait_ge(slot_in[slot], value)
                pe.wait_ge(hidT_ok, e + 1)
                down(slot).then_inc(y_pe, 1)

            def expert(e, odd):
                h16 = 8 * (e - 1) if odd else 8 * e
                pe.wait_ge(sel_low, 2 * e + 2)
                gate_up(e)
                if not (isinstance(e, int) and e == E - 1):
                    sel(e + 1, 0 if odd else 1, h16 + 32 if odd else h16 + 16)
                if not (isinstance(e, int) and e == 1):
                    pe.wait_ge(y_ok, 2 * e - 2)
                down_rows(e - 1, 2 if odd else 5, h16 + 16)
                hidden(e)

            sel(0, 0, 16)
            pe.wait_ge(gate2_ok, 2)
            pe.wait_ge(sel_low, 2)
            gate_up(0)
            sel(1, 1, 16)
            hidden(0)
            expert(1, True)
            expert(2, False)
            with pe.Fori(LOOP, E - 1, 2) as e:
                expert(e, True)
                expert(e + 1, False)
            expert(E - 1, True)
            pe.wait_ge(y_ok, 2 * E - 2)
            down_rows(E - 1, 5, 8 * (E + 2))

            pe.wait_ge(over_ok, 1)
            n_over = pe.value_load(over_n[0:1, 0:1], min_val=0, max_val=MOST_OVER)
            with pe.If(n_over > 0):
                with pe.Fori(0, n_over) as o:
                    pe.wait_ge(o_order, STEPS_OVER * o + 2 * NT + 2)
                    for t in range(NT):
                        for i in range(2):
                            last = mm(bank[7][:, 0:1], over_hot[:, t, :], tok_id[:, t, i:i + 1],
                                      start=t == 0 and i == 0, stop=t == NT - 1 and i == 1)
                    last.then_inc(o_idx_pe, 1)
                    pe.wait_ge(o_gathered, 16 * o + 16)
                    for k in range(KD):
                        last = nc.tensor.transpose(bank[5 + k // 4][:, (k % 4) * P:(k % 4 + 1) * P],
                                                   xg[0][:, k * P:(k + 1) * P], ident[:])
                    last.then_inc(o_sel_pe, 1)
                    pe.wait_ge(o_sel, 2 * o + 2)
                    pe.wait_ge(o_w, 48 * o + 48)
                    for k in range(KD):
                        for h in range(2):
                            last = mm(bank[h][:], over_selT[:, k, :], ring_k[k // 4][:, k % 4, h * F:(h + 1) * F],
                                      start=k == 0, stop=k == KD - 1)
                    last.then_inc(o_gu, 1)
                    pe.wait_ge(o_hid, o + 1)
                    for k in range(KF):
                        last = nc.tensor.transpose(bank[4][:, k * P:(k + 1) * P], hid[:, k * P:(k + 1) * P], ident[:])
                    last.then_inc(o_hidT_pe, 1)
                    pe.wait_ge(o_hidT, o + 1)
                    down(2).then_inc(o_y_pe, 1)


_INS = ['x', 'c', 'w_in', 'conv_w', 'pool_w', 'pool_scale', 'w_out', 'norm1_g', 'norm2_g',
        'w_ada', 'b_ada', 'w_router', 'router_bias', 'w_gate_up', 'w_down', 'final_g']
_OUTS = [((1, 512, 1024), 'float32')]


def kernel(**inputs):
    import numpy as _np
    import concourse.bacc as _bacc
    from concourse import mybir as _mybir
    from concourse.bass_utils import run_bass_kernel_spmd as _run

    nc = _bacc.Bacc("TRN2", target_bir_lowering=False, num_devices=1)
    arrays, args = {}, []
    for name in _INS:
        a = _np.ascontiguousarray(inputs[name])
        arrays[f"in_{name}_dram"] = a
        args.append(nc.dram_tensor(f"in_{name}_dram", a.shape, _mybir.dt.from_np(a.dtype), kind="ExternalInput").ap())
    for i, (shape, dtype) in enumerate(_OUTS):
        dt = _mybir.dt.from_np(_np.dtype(dtype))
        args.append(nc.dram_tensor(f"out_{i}_dram", shape, dt, kind="ExternalOutput").ap())
    hybrid_block(nc, *args)
    r = _run(nc, [arrays], core_ids=[0])
    return r.results[0]["out_0_dram"]
```

```python
from contextlib import ExitStack

import concourse.bass as bass
from concourse import mybir

F32 = mybir.dt.float32
F32R = mybir.dt.float32r
BF16 = mybir.dt.bfloat16
U32 = mybir.dt.uint32
I32 = mybir.dt.int32
ALU = mybir.AluOpType
ACT = mybir.ActivationFunctionType
AX_X = mybir.AxisListType.X

P = 128
EPS = 1e-6
BIG = 1e30


def hybrid_block(nc, x, c, w_in, conv_w, pool_w, pool_scale, w_out, norm1_g, norm2_g,
                 w_ada, b_ada, w_router, router_bias, w_gate_up, w_down, final_g, out):
    T, D = x.shape[1], x.shape[2]
    NT, KD = T // P, D // P
    CW = conv_w.shape[2]
    NC = CW // P
    NG = pool_w.shape[1]
    WINDOWS = [2 << g for g in range(NG)]
    PAD = WINDOWS[-1]
    TAPS = conv_w.shape[1]
    E = w_router.shape[1]
    GRP = 4
    EG = E // GRP
    F = w_down.shape[2]
    KF = F // P
    HALF = D // 2
    PIECE = 4 * D
    MAIN = E * P
    MOST_OVER = 2 * T // P - 1

    ctx = ExitStack()
    with ctx:
        def sb(name, shape, dt=F32):
            return ctx.enter_context(nc.sbuf_tensor(name, shape, dt))

        def sem(name):
            return ctx.enter_context(nc.semaphore(name))

        bank = [ctx.enter_context(nc.psum_tensor(f"bank{i}", [P, HALF], F32)) for i in range(8)]

        ring = sb("ring", [P, 6, PIECE])
        x_sb = sb("x_sb", [P, NT, D])
        high = sb("high", [P, KD * T + D], F32R)
        low = sb("low", [P, KD * T + D], F32R)
        work = sb("work", [P, 3 * F])
        yT = sb("yT", [P, KD, T])
        acc = sb("acc", [P, 2, D])
        gate_bc = sb("gate_bc", [P, D])
        scale2_bc = sb("scale2_bc", [P, D])
        shift2_bc = sb("shift2_bc", [P, D])
        mixbuf = sb("mixbuf", [P, 4 * (PAD + T)])
        ident = sb("ident", [P, P])
        ones = sb("ones", [P, P])
        before = sb("before", [P, P], BF16)
        ones_h = sb("ones_h", [P, P], BF16)
        prm = sb("prm", [32, P])
        prmT = sb("prmT", [P, 32])
        c_act = sb("c_act", [P, KD])
        mod1 = sb("mod1", [P, 2, KD])
        icnt = sb("icnt", [P, PAD])
        stat = sb("stat", [P, 4, NT])
        squares = sb("squares", [P, D], BF16)
        root_warm = sb("root_warm", [P, 1])
        wr = sb("wr", [P, KD, E])
        bias_bc = sb("bias_bc", [P, E])
        iota_1 = sb("iota_1", [P, P], BF16)
        tok_id = sb("tok_id", [P, NT, 2], BF16)
        iota_e = sb("iota_e", [P, E])
        desc = sb("desc", [P, GRP])
        idx_main = sb("idx_main", [P, E], U32)
        idx_over = sb("idx_over", [P, 1], U32)
        slot_u = sb("slot_u", [P, 2, NT], U32)
        slot_main = sb("slot_main", [P, 2, NT], U32)
        over_n = sb("over_n", [P, 2], I32)

        vpad, sum_a, sum_b, gpad = (mixbuf[:, i * (PAD + T):(i + 1) * (PAD + T)] for i in range(4))
        SHORT, LONG = 12, 9
        route = ([mixbuf[:, 2 * D:2 * D + NT * E]] + [work[:, i * NT * E:(i + 1) * NT * E] for i in range(1, SHORT)]
                 + [mixbuf[:, D + i * NT * E:D + (i + 1) * NT * E] for i in range(LONG)])
        tail = mixbuf[:, D + LONG * NT * E:2 * D]
        combine = tail[:, 0:2 * NT].rearrange("p (i t) -> p i t", i=2)
        over_rel = tail[:, 2 * NT:4 * NT].rearrange("p (i t) -> p i t", i=2)
        over_sum, over_cmp = tail[:, E:2 * E], tail[:, 2 * E:3 * E]
        over_k, over_e = tail[:, 3 * E:3 * E + 1], tail[:, 3 * E + 1:3 * E + 2]

        yflat = yT[:, :, :].rearrange("p k t -> p (k t)")
        onehot = yflat[:, 0:T * E // 2].bitcast(BF16).rearrange("p (t e j) -> p t e j", t=NT, e=E)
        over_selT = yflat[:, 0:D].rearrange("p (k j) -> p k j", k=KD)
        over_hot = yflat[:, D:D + NT * P // 2].bitcast(BF16).rearrange("p (t j) -> p t j", t=NT)
        final_bc = yflat[:, 3 * D:4 * D]
        xg = [scale2_bc[:, :], shift2_bc[:, :]]
        y_sb = [acc[:, 0, :], acc[:, 1, :]]
        silu_g, hid = work[:, 0:F], work[:, F:2 * F]
        hidT = work[:, 2 * F:3 * F].rearrange("p (k j) -> p k j", k=KF)
        pool_w_sb = work[:, 0:NG * P].rearrange("p (g d) -> p g d", g=NG)
        h2 = [mixbuf[:, 0:D], mixbuf[:, D:2 * D], work[:, 0:D], mixbuf[:, 0:D]]
        gated = work[:, D:D + HALF]
        scoreT = yflat[0:E, 0:T]
        h2T = acc[:, 0, :].rearrange("p (k j) -> p k j", k=KD)
        hT = [part[:, 0:KD * T].rearrange("p (k t) -> p k t", k=KD) for part in (high, low)]
        wsplit = [part[:, KD * T:].rearrange("p (b k m) -> p b k m", b=2, k=4) for part in (high, low)]
        wchunk = [part[:, 0:KD * T].rearrange("p (b n) -> p b n", b=4) for part in (high, low)]
        xselT = [part[:, KD * T:].rearrange("p (k j) -> p k j", k=KD) for part in (high, low)]
        as_f32 = lambda ap: ap.bitcast(F32)
        ring_k = [ring[:, s, :].rearrange("p (k n) -> p k n", k=4) for s in range(6)]
        ring_w = [ring[:, s, :].rearrange("p (k n) -> p k n", k=KD) for s in range(6)]
        wout_k = [ring_k[2 + k // 4][:, k % 4, :] for k in range(KD)]
        y_low, y_high, res = ([ring_k[slot][:, t, :] for t in range(NT)] for slot in (3, 4, 5))

        h2_dram = nc.dram_tensor("h2_rows", [T, D], F32)
        y_dram = nc.dram_tensor("y_rows", [MAIN + MOST_OVER * P, D], F32)

        prm_in, wr_in, bias_in, poolw_in, norm2_in, final_in = (
            sem(n) for n in ("prm_in", "wr_in", "bias_in", "poolw_in", "norm2_in", "final_in"))
        ada1_in = [sem(f"ada1_in{i}") for i in range(8)]
        x_in = [sem(f"x_in{t}") for t in range(NT)]
        win_in = [[sem(f"win_in{i}{half}") for half in range(2)] for i in range(4)]
        ada2_in = [sem(f"ada2_in{i}") for i in range(8)]
        wout_in = sem("wout_in")
        slot_in = [sem(f"slot_in{i}") for i in range(6)]
        brow_in = [sem(f"brow_in{i}") for i in range(6)]
        const_ok, acc_zero, pads_ok, pool_order = (sem(n) for n in ("const_ok", "acc_zero", "pads_ok", "pool_order"))
        prmT_pe, prmT_ok, cact_ok, ada_ok, acc_used = (
            sem(n) for n in ("prmT_pe", "prmT_ok", "cact_ok", "ada_ok", "acc_used"))
        sq_ok, ms_ok, root_ok, rstd_ok, xn_ok, xT_pe, xT_ok = (
            sem(n) for n in ("sq_ok", "ms_ok", "root_ok", "rstd_ok", "xn_ok", "xT_pe", "xT_ok"))
        mod1_ok, half_done, act_ev, dve_ev = (
            sem(n) for n in ("mod1_ok", "half_done", "act_ev", "dve_ev"))
        pooled_ok, pool_pe, pool_ev, bc_pe, bc_ev, scale_ok = (
            sem(n) for n in ("pooled_ok", "pool_pe", "pool_ev", "bc_pe", "bc_ev", "scale_ok"))
        x2_ok, sq2_ok, ms2_ok, root2_ok, rstd2_ok, h2_ok = (
            sem(n) for n in ("x2_ok", "sq2_ok", "ms2_ok", "root2_ok", "rstd2_ok", "h2_ok"))
        h2T_pe, h2T_ok, logit_pe, score_ok, score_pe = (
            sem(n) for n in ("h2T_pe", "h2T_ok", "logit_pe", "score_ok", "score_pe"))
        h2_stored = [sem(f"h2_stored{t}") for t in range(NT)]
        hT_full, rhs_high, rhs_low, lhs_high, lhs_low = (
            sem(n) for n in ("hT_full", "rhs_high", "rhs_low", "lhs_high", "lhs_low"))
        gu_high, gu_low, chunk_pe, sel_low = (sem(n) for n in ("gu_high", "gu_low", "chunk_pe", "sel_low"))
        mask_ok, rank_pe, rank_ev, hot_ok, idx_pe, idx_ok, slots_ok, over_ok = (
            sem(n) for n in ("mask_ok", "rank_pe", "rank_ev", "hot_ok", "idx_pe", "idx_ok", "slots_ok", "over_ok"))
        gate2_pe, gate2_ok = sem("gate2_pe"), sem("gate2_ok")
        icnt_ok, filled = sem("icnt_ok"), sem("filled")
        order = sem("vector_order")
        gathered = [sem("gathered0"), sem("gathered1")]
        stored = [sem("stored0"), sem("stored1")]
        sel_pe, sel_ok, silu_ok, hid_ok, hidT_pe, hidT_ok, y_pe, y_ok = (
            sem(n) for n in ("sel_pe", "sel_ok", "silu_ok", "hid_ok", "hidT_pe",
                             "hidT_ok", "y_pe", "y_ok"))
        o_pick, o_idx_pe, o_idx, o_sel_pe, o_sel, o_w, o_gu, o_silu, o_hid, o_hidT_pe, o_hidT, o_y_pe, o_y = (
            sem("over_" + n) for n in ("pick", "idx_pe", "idx", "sel_pe", "sel", "w", "gu", "silu",
                                       "hid", "hidT_pe", "hidT", "y_pe", "y"))
        o_gathered, o_stored, o_order, o_seen = (sem("over_" + n) for n in ("gathered", "stored", "order", "seen"))
        last_stored, low_rows, all_rows, fin_rstd, fin_stat, fin_sq, fin_root, res_ok, out_in = (
            sem(n) for n in ("last_stored", "low_rows", "all_rows", "fin_rstd", "fin_stat", "fin_sq", "fin_root",
                             "res_ok", "out_in"))
        again = sem("again")
        low_in = [sem(f"low_in{t}") for t in range(NT)]
        high_in = [sem(f"high_in{t}") for t in range(NT)]

        tiles = [("v", g) for g in range(NG)] + [(m, i) for i in range(NC) for m in ("C", "h", "B")]
        GROUP = {"B": 0, "C": 1, "h": 2, "v": 3}
        WSLOT = {"v": 4, "C": 5, "h": 0, "B": 1}
        WORDER = ["v", "C", "h", "B"]
        n_act = n_dve = 0
        freed = []
        for m, _ in tiles:
            if m in ("v", "C"):
                n_act += 1
                freed.append((act_ev, n_act))
            else:
                n_dve += 1
                freed.append((dve_ev, n_dve))
        ADA_SLOTS = [(0, 1), (2, 3), (2, 3), (4, 2), (3, 4), (0, 1)]
        REDUCE_AFTER = {9: 2, 11: 3, 14: 4}
        ADA_FROM, ADA_PER = 5, 3
        BEFORE_MIX = 24

        NP, NM = len(tiles), 2 * NT
        MIX_ORDER = list(range(NC, KD)) + list(range(NC))

        def lhs_half(b):
            n, half = b // 2, b % 2
            if n < NP:
                m, i = tiles[n]
                return ring_w[WSLOT[m]][:, 4 * half:4 * half + 4, i * P:(i + 1) * P]
            k, t = MIX_ORDER[4 * half], (n - NP) % NT
            return yT[:, k:k + 4, t * P:(t + 1) * P]

        def wout_half(h, i):
            return wout_k[MIX_ORDER[i]][:, h * HALF:(h + 1) * HALF]

        block = ctx.enter_context(nc.Block())
        LOOP = 3
        BATCHES = [(0, 2), (2, 4), (4, 8), (8, 12), (12, E)]
        STEPS_OVER = 2 * NT + 4

        def gate_up_place(e, odd):
            if isinstance(e, int) and e == 0:
                return (4, 5), [(slot_in[4], 16), (slot_in[5], 16)]
            if odd:
                return (0, 1), [(slot_in[0], 8 * e + 8), (slot_in[1], 8 * e + 8)]
            return (3, 4), [(slot_in[3], 8 * e), (slot_in[4], 8 * e + 16)]

        @block.sync
        def _(sp):
            def ada(j, half, to, signals, ks):
                src = w_ada[0, half * 4 * P:(half * 4 + 4) * P, j * D:(j + 1) * D].rearrange("(k p) n -> p k n", p=P)
                for q in range(0, 4, ks):
                    sp.dma_start(ring_k[to][:, q:q + ks, :], src[:, q:q + ks, :]).then_inc(signals[q // ks], 16)

            rows = 2 * KD
            sp.dma_start(prm[0:KD, :], c.rearrange("b (k p) -> (b k) p", p=P)).then_inc(prm_in, 16)
            sp.dma_start(prm[KD:rows, :], norm1_g.rearrange("b (k p) -> (b k) p", p=P)).then_inc(prm_in, 16)
            sp.dma_start(prm[rows:rows + TAPS * NC, :],
                         conv_w.rearrange("l k (i p) -> (l k i) p", p=P)).then_inc(prm_in, 16)
            sp.dma_start(prm[rows + TAPS * NC:32, :], pool_scale.rearrange("l (i p) -> (l i) p", p=P)).then_inc(prm_in, 16)
            for t in range(NT):
                sp.dma_start(x_sb[:, t, :], x[0, t * P:(t + 1) * P, :]).then_inc(x_in[t], 16)
            ada(0, 0, 0, ada1_in[0:2], 2)
            ada(0, 1, 1, ada1_in[2:4], 2)
            ada(1, 0, 2, ada1_in[4:6], 2)
            ada(1, 1, 3, ada1_in[6:8], 2)
            for n, m in enumerate(WORDER):
                if m == "h":
                    sp.wait_ge(ada_ok, 4)
                if m == "B":
                    sp.wait_ge(ada_ok, 8)
                g = GROUP[m]
                for half in range(2):
                    sp.dma_start(ring_w[WSLOT[m]][:, 4 * half:4 * half + 4, :],
                                 w_in[0, half * 4 * P:(half + 1) * 4 * P, g * CW:(g + 1) * CW]
                                 .rearrange("(k p) n -> p k n", p=P)).then_inc(win_in[n][half], 16)
            for j in range(2, 5):
                for half in range(2):
                    n = 2 * (j - 2) + half
                    if n == 2:
                        sp.wait_ge(lhs_low, 2 * NG)
                    else:
                        sp.wait_ge(ada_ok, {0: 12, 1: 16}.get(n, 4 * (n + 2)))
                    ada(j, half, ADA_SLOTS[j][half], [ada2_in[n]], 4)
            for half in range(2):
                sp.wait_ge(ada_ok, (32, 36)[half])
                sp.dma_start(ring_k[2 + half][:, :, :], w_out[0, half * 4 * P:(half + 1) * 4 * P, :]
                             .rearrange("(k p) n -> p k n", p=P)).then_inc(wout_in, 16)

            def gate_up(e, half, to):
                src = w_gate_up[0, bass.ds(e, 1), half * 4 * P:(half * 4 + 4) * P, :]
                sp.dma_start(ring_k[to][:, :, :], src.rearrange("a (k p) n -> p (a k) n", p=P)).then_inc(slot_in[to], 16)

            def down(e, to):
                src = w_down[0, bass.ds(e, 1)]
                sp.dma_start(ring_k[to][:, :, :], src.rearrange("a (k p) n -> p (a k) n", p=P)).then_inc(slot_in[to], 16)

            sp.wait_ge(ada_ok, 40)
            gate_up(0, 0, 4)
            sp.wait_ge(lhs_low, 2 * NP)
            gate_up(0, 1, 5)
            ada(5, 0, 0, [ada2_in[6]], 4)
            ada(5, 1, 1, [ada2_in[7]], 4)
            sp.wait_ge(ada_ok, 44)
            gate_up(1, 0, 0)
            sp.wait_ge(rhs_low, 3 * KD)
            down(0, 2)
            gate_up(2, 0, 3)
            sp.wait_ge(ada_ok, 48)
            gate_up(1, 1, 1)
            sp.wait_ge(gu_low, 4)
            for i in range(2):
                sp.wait_ge(gathered[i], 16)
            gate_up(2, 1, 4)
            sp.wait_ge(gu_low, 8)
            down(1, 5)

            def refill(e, s):
                sp.wait_ge(gu_low, 8 * e - 12)
                gate_up(e, 0, s)
                sp.wait_ge(gu_low, 8 * e - 8)
                gate_up(e, 1, s + 1)
                sp.wait_ge(y_pe, e - 2)
                down(e - 1, s + 2)

            with sp.Fori(LOOP, E - 1, 2) as e:
                refill(e, 0)
                refill(e + 1, 3)
            refill(E - 1, 0)
            sp.wait_ge(y_pe, E - 2)
            down(E - 1, 5)

            for h in range(2):
                sp.wait_ge(y_ok, 2 * E - 1 + h)
                sp.dma_start(y_dram[(E - 1) * P:E * P, h * HALF:(h + 1) * HALF],
                             y_sb[(E - 1) % 2][:, h * HALF:(h + 1) * HALF]).then_inc(last_stored, 16)

            sp.wait_ge(over_ok, 1)
            n_over = sp.value_load(over_n[0:1, 0:1], min_val=0, max_val=MOST_OVER)
            sp.wait_ge(y_pe, E + 1)
            with sp.If(n_over > 0):
                for lo in range(0, MOST_OVER, NT):
                    n = min(NT, MOST_OVER - lo)
                    sp.dma_start(y_dram[MAIN + lo * P:MAIN + (lo + n) * P, :].rearrange("(t p) d -> p t d", p=P),
                                 x_sb[:, 0:n, :]).then_inc(filled, 16)
                with sp.Fori(0, n_over) as o:
                    sp.wait_ge(o_pick, o + 1)
                    sp.sem_inc(o_seen, 1)
                    ex = sp.value_load(over_n[0:1, 1:2], min_val=0, max_val=E - 1)
                    for half in range(2):
                        src = w_gate_up[0, bass.ds(ex, 1), half * 4 * P:(half * 4 + 4) * P, :]
                        sp.dma_start(ring_k[half][:, :, :], src.rearrange("a (k p) n -> p (a k) n", p=P)).then_inc(o_w, 16)
                    sp.dma_start(ring_k[2][:, :, :],
                                 w_down[0, bass.ds(ex, 1)].rearrange("a (k p) n -> p (a k) n", p=P)).then_inc(o_w, 16)

            for n in range(2 * NT):
                t, cols = n // 2, slice(n % 2 * HALF, (n % 2 + 1) * HALF)
                sp.wait_ge(res_ok, n + 1)
                sp.dma_start(out[0, t * P:(t + 1) * P, cols], res[t][:, cols]).then_inc(out_in, 16)
            sp.wait_ge(out_in, 32 * NT)

        @block.gpsimd
        def _(pool):
            nc.gpsimd.memset(ident[:], 0.0).then_inc(pool_order, 1)
            nc.gpsimd.memset(acc[:, 0, :], 0.0).then_inc(acc_zero, 1)
            pool.wait_ge(pool_order, 1)
            nc.gpsimd.affine_select(out=ident[:], in_=ident[:], compare_op=ALU.not_equal, fill=1.0, base=0,
                                    pattern=[[-1, P]], channel_multiplier=1).then_inc(const_ok, 1)
            nc.gpsimd.memset(acc[:, 1, :], 0.0).then_inc(acc_zero, 1)
            for j in range(2):
                pool.wait_ge(acc_zero, j + 1)
                pool.dma_start(acc[0:1, j, :], b_ada[:, j * D:(j + 1) * D]).then_inc(brow_in[j], 16)
            nc.gpsimd.memset(ones[:], 1.0).then_inc(const_ok, 1)
            nc.gpsimd.memset(vpad[:, 0:PAD], 0.0).then_inc(pads_ok, 1)
            nc.gpsimd.memset(gpad[:, 0:TAPS - 1], 0.0).then_inc(pads_ok, 1)
            iota = lambda to, pattern, base, step: nc.gpsimd.iota(
                to, pattern=pattern, base=base, channel_multiplier=step, allow_small_or_imprecise_dtypes=True)
            iota(icnt[:], [[1, PAD]], 1, 0).then_inc(pads_ok, 1)
            nc.gpsimd.memset(before[:], 1.0).then_inc(pool_order, 1)
            pool.wait_ge(pool_order, 2)
            nc.gpsimd.affine_select(out=before[:], in_=before[:], compare_op=ALU.is_gt, fill=0.0, base=0,
                                    pattern=[[1, P]], channel_multiplier=-1).then_inc(const_ok, 1)
            nc.gpsimd.memset(ones_h[:], 1.0).then_inc(const_ok, 1)
            iota(iota_1[:], [[1, P]], 1, 0).then_inc(const_ok, 1)
            iota(iota_e[:], [[1, E]], 0, 0).then_inc(const_ok, 1)
            iota(desc[:], [[-1, GRP]], GRP, 0).then_inc(const_ok, 1)
            iota(tok_id[:, :, 0], [[0, NT]], 0, 1).then_inc(const_ok, 1)
            iota(tok_id[:, :, 1], [[P, NT]], 0, 0).then_inc(const_ok, 1)

            def bias_row(j):
                pool.wait_ge(*((acc_used, j - 1) if j < 4 else (bc_pe, j - 3)))
                nc.gpsimd.memset(acc[:, j % 2, :], 0.0).then_inc(acc_zero, 1)
                pool.wait_ge(acc_zero, j + 1)
                pool.dma_start(acc[0:1, j % 2, :], b_ada[:, j * D:(j + 1) * D]).then_inc(brow_in[j], 16)

            bias_row(2)
            for n in range(NP + NM):
                for b in (2 * n, 2 * n + 1):
                    pool.wait_ge(lhs_high, b + 1)
                    nc.gpsimd.tensor_tensor(wsplit[1][:, b % 2], lhs_half(b), as_f32(wsplit[0][:, b % 2]),
                                            ALU.subtract).then_inc(lhs_low, 1)
                if n == 0:
                    bias_row(3)
                if n - 1 in REDUCE_AFTER and REDUCE_AFTER[n - 1] < 4:
                    bias_row(REDUCE_AFTER[n - 1] + 2)
            for t in range(NT):
                pool.wait_ge(h2_ok, 2 * t + 2)
                pool.dma_start(h2_dram[t * P:(t + 1) * P, :], h2[t]).then_inc(h2_stored[t], 16)
            for k in range(4):
                pool.wait_ge(gu_high, k + 1)
                nc.gpsimd.tensor_tensor(wchunk[1][:, k], ring_k[4][:, k, :], as_f32(wchunk[0][:, k]),
                                        ALU.subtract).then_inc(gu_low, 1)
            for t in range(NT):
                pool.wait_ge(h2_stored[t], 16)

            def gather(idx, to, signal):
                pool.indirect_dma_start(out=to, out_offset=None, in_=h2_dram[:, :],
                                        in_offset=bass.IndirectOffsetOnAxis(ap=idx, axis=0)).then_inc(signal, 16)

            def store(e):
                pool.wait_ge(y_ok, 2 * (e + 1))
                pool.dma_start(y_dram[e * P:(e + 1) * P, :], y_sb[e % 2]).then_inc(stored[e % 2], 16)

            for e in range(2):
                pool.wait_ge(idx_ok, 1)
                gather(idx_main[:, e:e + 1], xg[e], gathered[e])
            for e in range(E):
                if e + 2 < E:
                    for b, (first, _) in enumerate(BATCHES):
                        if e + 2 == first:
                            pool.wait_ge(idx_ok, b + 1)
                    pool.wait_ge(sel_pe, e + 1)
                    gather(idx_main[:, e + 2:e + 3], xg[e % 2], gathered[e % 2])
                if e >= 2:
                    store(e - 2)
            def rows_of(i, slots, source, signal, first=0, end=NT):
                for t in range(first, end):
                    pool.indirect_dma_start(out=(y_low, y_high)[i][t], out_offset=None, in_=source,
                                            in_offset=bass.IndirectOffsetOnAxis(ap=slots[:, i, t:t + 1], axis=0)
                                            ).then_inc(signal(t), 16)

            store(E - 2)
            pool.wait_ge(slots_ok, 1)
            for i in range(2):
                pool.wait_ge(stored[i], 16 * (E // 2 - i))
            pool.wait_ge(gu_low, 8 * (E - 1))
            rows_of(0, slot_main, y_dram[0:(E - 1) * P, :], lambda t: low_in[t], 0, 2)
            pool.wait_ge(y_ok, 2 * E)
            rows_of(0, slot_main, y_dram[0:(E - 1) * P, :], lambda t: low_in[t], 2, NT)
            pool.wait_ge(last_stored, 32)
            rows_of(1, slot_main, y_dram[0:MAIN, :], lambda t: high_in[t])

            pool.wait_ge(over_ok, 1)
            n_over = pool.value_load(over_n[0:1, 0:1], min_val=0, max_val=MOST_OVER)
            with pool.If(n_over > 0):
                pool.wait_ge(filled, 32)
                with pool.Fori(0, n_over) as o:
                    pool.wait_ge(o_idx, o + 1)
                    pool.sem_inc(o_seen, 1)
                    gather(idx_over[:, 0:1], xg[0], o_gathered)
                    pool.wait_ge(o_y, 2 * o + 2)
                    pool.dma_start(y_dram[bass.ds(MAIN + o * P, P), :], y_sb[0]).then_inc(o_stored, 16)
                    pool.wait_ge(o_stored, 16 * o + 16)
                for t in range(NT):
                    pool.wait_ge(low_in[t], 16)
                    pool.wait_ge(high_in[t], 16)
                for i in range(2):
                    rows_of(i, slot_u, y_dram[:, :], lambda t: again)

        @block.scalar
        def _(act):
            rows = 2 * KD
            act.dma_start(pool_w_sb, pool_w[0].rearrange("g c d -> c g d")).then_inc(poolw_in, 16)
            act.dma_start(wr[:, :, :], w_router.rearrange("(k p) e -> p k e", p=P)).then_inc(wr_in, 16)
            act.dma_start(bias_bc[:, :], router_bias.rearrange("(a e) -> a e", a=1).to_broadcast([P, E])).then_inc(bias_in, 16)
            act.dma_start(scale2_bc[:, :], norm2_g.to_broadcast([P, D])).then_inc(norm2_in, 16)

            act.wait_ge(prmT_ok, 1)
            nc.scalar.activation(c_act[:], prmT[:, 0:KD], ACT.Silu).then_inc(cact_ok, 1)
            for t in range(NT):
                act.wait_ge(x_in[t], 16)
                nc.scalar.activation(yflat[:, t * D:(t + 1) * D], x_sb[:, t, :], ACT.Square,
                                     accum_out=stat[:, 0, t:t + 1]).then_inc(sq_ok, 1)
            act.wait_ge(ms_ok, 1)
            nc.scalar.activation(stat[:, 1, :], stat[:, 3, :], ACT.Sqrt).then_inc(root_ok, 1)
            act.wait_ge(rstd_ok, 1)
            act.wait_ge(sq_ok, NT)
            for t in range(NT):
                nc.scalar.activation(yflat[:, t * D:(t + 1) * D], x_sb[:, t, :], ACT.Copy,
                                     scale=stat[:, 2, t:t + 1]).then_inc(xn_ok, 1)
            act.wait_ge(xT_pe, KD)
            for k in range(KD):
                nc.scalar.activation(yT[:, k, :], bank[k][:], ACT.Copy).then_inc(xT_ok, 1)

            def split_half(b):
                if b < 2 * NP and tiles[b // 2][1] == 0:
                    act.wait_ge(win_in[WORDER.index(tiles[b // 2][0])][b % 2], 16)
                if b >= 2:
                    act.wait_ge(half_done, b - 1)
                nc.scalar.activation(wsplit[0][:, b % 2], lhs_half(b), ACT.Copy).then_inc(lhs_high, 1)

            for b in range(2):
                split_half(b)
            for k in range(KD):
                act.wait_ge(hT_full, k + 1)
                nc.scalar.activation(hT[0][:, k, :], yT[:, k, :], ACT.Copy).then_inc(rhs_high, 1)

            def evacuate(n):
                m, i = tiles[n]
                if m == "v":
                    act.wait_ge(half_done, 2 * n + 2)
                    if i == 0:
                        act.wait_ge(pads_ok, 3)
                    else:
                        act.wait_ge(pooled_ok, i)
                    nc.scalar.activation(vpad[:, PAD:], bank[n % 4][:], ACT.Copy).then_inc(act_ev, 1)
                if m == "C":
                    if i == 0:
                        act.wait_ge(pooled_ok, NG)
                    else:
                        act.wait_ge(dve_ev, 2 * i - 1)
                    act.wait_ge(half_done, 2 * n + 2)
                    nc.scalar.activation(sum_a[:, 0:T], bank[n % 4][:], ACT.Copy).then_inc(act_ev, 1)

            def after(n):
                evacuate(n)
                if 2 <= n <= NG + 1:
                    g = n - 2
                    act.wait_ge(pool_pe, g + 1)
                    o = rows + TAPS * NC + g
                    nc.scalar.activation(yT[:, NC + g, :], bank[4 + g % 2][:], ACT.Copy,
                                         scale=prmT[:, o:o + 1]).then_inc(pool_ev, 1)
                j = REDUCE_AFTER.get(n)
                if j in (2, 3):
                    act.wait_ge(bc_pe, j - 1)
                    for h in range(2):
                        nc.scalar.activation((gate_bc if j == 2 else shift2_bc)[:, h * HALF:(h + 1) * HALF],
                                             bank[6 + h][:], ACT.Copy).then_inc(bc_ev, 1)

            for n, (m, i) in enumerate(tiles):
                if n:
                    for b in (2 * n, 2 * n + 1):
                        split_half(b)
                    after(n - 1)
            after(NP - 1)

            def split_out(h):
                for half in range(2):
                    if h == 0 and half == 0:
                        act.wait_ge(pool_ev, NG)
                        act.wait_ge(wout_in, 32)
                    if h == 0 and half == 1:
                        act.wait_ge(dve_ev, 2 * NC)
                    split_half(2 * (NP + h * NT) + half)
                    act.wait_ge(half_done, 2 * (NP + h * NT) - 1 + half)
                    for i in range(4 * half, 4 * half + 4):
                        nc.scalar.activation(hT[0][:, i, :], wout_half(h, i), ACT.Copy).then_inc(rhs_high, 1)

            for h in range(2):
                split_out(h)
                for t in range(1, NT - h * (NT - 1)):
                    for b in range(2 * (NP + t), 2 * (NP + t) + 2):
                        split_half(b)

            def split(e, chunks, slots, waits=None):
                for k in chunks:
                    if k % 4 == 0:
                        act.wait_ge(*waits[k // 4])
                    if not (isinstance(e, int) and e == 0 and k < 4):
                        act.wait_ge(chunk_pe, 8 * e + k - 3)
                    nc.scalar.activation(wchunk[0][:, k % 4], ring_k[slots[k // 4]][:, k % 4, :],
                                         ACT.Copy).then_inc(gu_high, 1)

            def h2T_copy(t):
                act.wait_ge(h2T_pe, t + 1)
                if t >= 1:
                    act.wait_ge(logit_pe, t)
                for h in range(2):
                    nc.scalar.activation(h2T[:, 4 * h:4 * h + 4, :].rearrange("p k j -> p (k j)"), bank[4 + h][:],
                                         ACT.Copy).then_inc(h2T_ok, 1)

            for t in range(NT):
                if t + 1 < NT:
                    for half in range(2):
                        split_half(2 * (NP + NT + t + 1) + half)
                act.wait_ge(x2_ok, NT + t + 1)
                if t:
                    act.wait_ge(sq2_ok, t)
                nc.scalar.activation(squares[:], x_sb[:, t, :], ACT.Square,
                                     accum_out=stat[:, 0, t:t + 1]).then_inc(sq2_ok, 1)
                if t >= 2:
                    h2T_copy(t - 2)
                if t:
                    act.wait_ge(ms2_ok, t)
                    lo = t if t > 1 else 0
                    nc.scalar.activation(stat[:, 1, lo:t + 1], stat[:, 3, lo:t + 1], ACT.Sqrt).then_inc(root2_ok, 1)
            for t in range(2, NT):
                h2T_copy(t)
                if t == 3:
                    act.wait_ge(logit_pe, NT)
                cols = slice((t - 2) * 2 * P, (t - 1) * 2 * P)
                nc.scalar.activation(scoreT[:, cols], bank[4 + t][0:E, cols], ACT.Sigmoid).then_inc(score_ok, 1)
            act.wait_ge(half_done, 2 * (NP + NM))
            split(0, range(4), *gate_up_place(0, False))
            act.wait_ge(gate2_pe, 1)
            for h in range(2):
                nc.scalar.activation(gate_bc[:, h * HALF:(h + 1) * HALF], bank[h][:], ACT.Copy).then_inc(gate2_ok, 1)

            def sel_copy(e):
                act.wait_ge(sel_pe, e + 1)
                for h in range(2):
                    nc.scalar.activation(xselT[0][:, 4 * h:4 * h + 4, :].rearrange("p k j -> p (k j)"), bank[5 + h][:],
                                         ACT.Copy).then_inc(sel_ok, 1)

            def silu(e):
                act.wait_ge(chunk_pe, 8 * e + 8)
                nc.scalar.activation(silu_g, bank[0][:], ACT.Silu).then_inc(silu_ok, 1)

            def hid_copy(e):
                act.wait_ge(hidT_pe, e + 1)
                nc.scalar.activation(hidT.rearrange("p k j -> p (k j)"), bank[4][:], ACT.Copy).then_inc(hidT_ok, 1)

            def expert(e, odd, last=False):
                split(e, range(4, KD), *gate_up_place(e, odd))
                silu(e)
                if not last:
                    sel_copy(e + 1)
                    split(e + 1, range(4), *gate_up_place(e + 1, not odd))
                hid_copy(e)

            sel_copy(0)
            for e in range(LOOP):
                expert(e, e % 2 == 1)
            with act.Fori(LOOP, E - 1, 2) as e:
                expert(e, True)
                expert(e + 1, False)
            expert(E - 1, True, last=True)

            act.wait_ge(over_ok, 1)
            n_over = act.value_load(over_n[0:1, 0:1], min_val=0, max_val=MOST_OVER)
            with act.If(n_over > 0):
                with act.Fori(0, n_over) as o:
                    act.wait_ge(o_sel_pe, o + 1)
                    for h in range(2):
                        nc.scalar.activation(over_selT[:, 4 * h:4 * h + 4, :].rearrange("p k j -> p (k j)"),
                                             bank[5 + h][:], ACT.Copy).then_inc(o_sel, 1)
                    act.wait_ge(o_gu, o + 1)
                    nc.scalar.activation(silu_g, bank[0][:], ACT.Silu).then_inc(o_silu, 1)
                    act.wait_ge(o_hidT_pe, o + 1)
                    nc.scalar.activation(hidT.rearrange("p k j -> p (k j)"), bank[4][:], ACT.Copy).then_inc(o_hidT, 1)

            act.wait_ge(idx_ok, len(BATCHES))
            act.dma_start(final_bc, final_g.rearrange("(a d) -> a d", a=1).to_broadcast([P, D])).then_inc(final_in, 16)
            nc.scalar.activation(root_warm[:], ones[:, 0:1], ACT.Sqrt)
            for t in range(NT):
                act.wait_ge(all_rows, t + 1)
                nc.scalar.activation(res[t], x_sb[:, t, :], ACT.Square, accum_out=stat[:, 0, t:t + 1]).then_inc(fin_sq, 1)
                if t % 2:
                    act.wait_ge(fin_stat, t // 2 + 1)
                    nc.scalar.activation(stat[:, 1, t - 1:t + 1], stat[:, 3, t - 1:t + 1], ACT.Sqrt).then_inc(fin_root, 1)

        @block.vector
        def _(dve):
            V = nc.vector
            count = [0]

            def link(ins):
                count[0] += 1
                ins.then_inc(order, 1)
                dve.wait_ge(order, count[0])

            def mean_square(cols, signal):
                V.tensor_scalar(stat[:, 3, cols], stat[:, 0, cols], 1.0 / D, EPS, ALU.mult, ALU.add).then_inc(signal, 1)

            def inverse_root(cols, signal):
                r, v, w = stat[:, 2, cols], stat[:, 3, cols], stat[:, 0, cols]
                link(V.reciprocal(r, stat[:, 1, cols]))
                link(V.tensor_tensor(w, r, r, ALU.mult))
                link(V.tensor_tensor(w, w, v, ALU.mult))
                link(V.tensor_scalar(w, w, -0.5, 1.5, ALU.mult, ALU.add))
                V.tensor_tensor(r, r, w, ALU.mult).then_inc(signal, 1)

            dve.wait_ge(prmT_pe, 1)
            V.tensor_copy(prmT[:], bank[7][:, 0:32]).then_inc(prmT_ok, 1)
            dve.wait_ge(cact_ok, 1)

            def ada(j, k):
                n = 8 * j + k
                if j < 2:
                    dve.wait_ge(ada1_in[n // 2], 16)
                else:
                    dve.wait_ge(ada2_in[(n - 16) // 4], 16)
                if k == 0:
                    dve.wait_ge(brow_in[j], 16)
                if n:
                    dve.wait_ge(ada_ok, n)
                V.scalar_tensor_tensor(out=acc[:, j % 2, :], in0=ring_k[ADA_SLOTS[j][k // 4]][:, k % 4, :],
                                       scalar=c_act[:, k:k + 1], in1=acc[:, j % 2, :],
                                       op0=ALU.mult, op1=ALU.add).then_inc(ada_ok, 1)

            dve.wait_ge(sq_ok, NT)
            mean_square(slice(0, NT), ms_ok)
            dve.wait_ge(pads_ok, 3)
            V.reciprocal(icnt[:], icnt[:]).then_inc(icnt_ok, 1)
            dve.wait_ge(ms_ok, 1)
            dve.wait_ge(root_ok, 1)
            inverse_root(slice(0, NT), rstd_ok)
            for j in range(2):
                for k in range(KD):
                    ada(j, k)
            dve.wait_ge(acc_used, 2)
            dve.wait_ge(prmT_ok, 1)
            V.tensor_copy(mod1[:, 0, :], bank[7][:, 0:KD]).then_inc(mod1_ok, 1)
            V.scalar_tensor_tensor(out=mod1[:, 1, :], in0=bank[7][:, KD:2 * KD], scalar=1.0, in1=prmT[:, KD:2 * KD],
                                   op0=ALU.add, op1=ALU.mult).then_inc(mod1_ok, 1)
            dve.wait_ge(mod1_ok, 2)

            def norm_low(k):
                dve.wait_ge(rhs_high, k + 1)
                V.tensor_tensor(hT[1][:, k, :], yT[:, k, :], as_f32(hT[0][:, k, :]), ALU.subtract).then_inc(rhs_low, 1)

            for k in range(KD):
                dve.wait_ge(xT_ok, k + 1)
                V.tensor_scalar(yT[:, k, :], yT[:, k, :], mod1[:, 1, k:k + 1], mod1[:, 0, k:k + 1],
                                ALU.mult, ALU.add).then_inc(hT_full, 1)
                if k:
                    norm_low(k - 1)
            norm_low(KD - 1)

            todo = [(j, k) for j in range(2, 6) for k in range(KD)]
            dve.wait_ge(icnt_ok, 1)

            def after(n):
                m, i = tiles[n]
                if m == "v":
                    dve.wait_ge(act_ev, i + 1)
                    src, win = vpad, WINDOWS[i]
                    for s in range(i + 1):
                        step, to = 1 << s, (sum_a, sum_b)[s % 2]
                        lo = 2 * step - 1
                        link(V.tensor_tensor(to[:, lo:], src[:, lo:], src[:, lo - step:PAD + T - step], ALU.add))
                        src = to
                    o = yT[:, NC + i, :]
                    link(V.tensor_tensor(o[:, 0:win], src[:, PAD:PAD + win], icnt[:, 0:win], ALU.mult))
                    link(V.tensor_tensor(o[:, 0:win], o[:, 0:win], vpad[:, PAD:PAD + win], ALU.subtract))
                    V.scalar_tensor_tensor(out=o[:, win:], in0=src[:, PAD + win:], scalar=1.0 / win,
                                           in1=vpad[:, PAD + win:], op0=ALU.mult, op1=ALU.subtract).then_inc(pooled_ok, 1)
                if m == "h":
                    dve.wait_ge(half_done, 2 * n + 2)
                    dve.wait_ge(act_ev, NG + i + 1)
                    V.tensor_tensor(gpad[:, TAPS - 1:TAPS - 1 + T], bank[n % 4][:], sum_a[:, 0:T],
                                    ALU.mult).then_inc(dve_ev, 1)
                    dve.wait_ge(dve_ev, 2 * i + 1)
                    tap = lambda k: prmT[:, 2 * KD + k * NC + i:2 * KD + k * NC + i + 1]
                    link(V.tensor_scalar(sum_b[:, 0:T], gpad[:, 0:T], tap(0), None, ALU.mult))
                    for k in range(1, TAPS):
                        link(V.scalar_tensor_tensor(out=sum_b[:, 0:T], in0=gpad[:, k:k + T], scalar=tap(k),
                                                    in1=sum_b[:, 0:T], op0=ALU.mult, op1=ALU.add))
                if m == "B":
                    dve.wait_ge(half_done, 2 * n + 2)
                    V.tensor_tensor(yT[:, i, :], bank[n % 4][:], sum_b[:, 0:T], ALU.mult).then_inc(dve_ev, 1)
                if REDUCE_AFTER.get(n) == 4:
                    dve.wait_ge(bc_pe, 3)
                    dve.wait_ge(norm2_in, 16)
                    for h in range(2):
                        part = scale2_bc[:, h * HALF:(h + 1) * HALF]
                        V.scalar_tensor_tensor(out=part, in0=bank[6 + h][:], scalar=1.0, in1=part,
                                               op0=ALU.add, op1=ALU.mult).then_inc(scale_ok, 1)

            for n in range(len(tiles)):
                if n:
                    after(n - 1)
                if n >= ADA_FROM:
                    for j, k in todo[:min(ADA_PER, len(todo) - (48 - 16 - BEFORE_MIX))]:
                        ada(j, k)
                    todo = todo[min(ADA_PER, len(todo) - (48 - 16 - BEFORE_MIX)):]
            after(len(tiles) - 1)

            def split_low(e, chunks, slots, waits=None):
                for k in chunks:
                    dve.wait_ge(gu_high, 8 * e + k + 1)
                    V.tensor_tensor(wchunk[1][:, k % 4], ring_k[slots[k // 4]][:, k % 4, :],
                                    as_f32(wchunk[0][:, k % 4]), ALU.subtract).then_inc(gu_low, 1)

            def split_out_low(h):
                for i in range(KD):
                    dve.wait_ge(rhs_high, KD * (1 + h) + i + 1)
                    V.tensor_tensor(hT[1][:, i, :], wout_half(h, i), as_f32(hT[0][:, i, :]),
                                    ALU.subtract).then_inc(rhs_low, 1)

            def residual(h, t):
                c, cols = h * NT + t, slice(h * HALF, (h + 1) * HALF)
                dve.wait_ge(half_done, 2 * (NP + c) + 2)
                if c:
                    dve.wait_ge(x2_ok, c)
                link(V.tensor_tensor(gated, bank[c % 4][:], gate_bc[:, cols], ALU.mult))
                V.tensor_tensor(x_sb[:, t, cols], x_sb[:, t, cols], gated, ALU.add).then_inc(x2_ok, 1)

            def norm2_mean(lo, hi):
                dve.wait_ge(sq2_ok, hi)
                mean_square(slice(lo, hi), ms2_ok)

            def norm2_root(n, lo, hi):
                dve.wait_ge(ms2_ok, n)
                dve.wait_ge(root2_ok, n)
                inverse_root(slice(lo, hi), rstd2_ok)
                dve.wait_ge(rstd2_ok, n)

            def norm2_rows(t, h):
                if t == NT - 1 and h == 0:
                    dve.wait_ge(h2T_pe, 1)
                    dve.wait_ge(h2_stored[0], 16)
                cols = slice(h * HALF, (h + 1) * HALF)
                link(V.scalar_tensor_tensor(out=h2[t][:, cols], in0=x_sb[:, t, cols], scalar=stat[:, 2, t:t + 1],
                                            in1=scale2_bc[:, cols], op0=ALU.mult, op1=ALU.mult))
                V.tensor_tensor(h2[t][:, cols], h2[t][:, cols], shift2_bc[:, cols], ALU.add).then_inc(h2_ok, 1)

            def ada_next(n):
                for j, k in todo[:n]:
                    ada(j, k)
                del todo[:n]

            dve.wait_ge(bc_ev, 4)
            dve.wait_ge(scale_ok, 2)
            split_out_low(0)
            for t, n in ((0, 2), (1, 2), (2, 1)):
                residual(0, t)
                ada_next(n)
            split_out_low(1)
            residual(0, NT - 1)
            residual(1, 0)
            ada_next(1)
            residual(1, 1)
            norm2_mean(0, 2)
            norm2_root(1, 0, 2)
            norm2_rows(0, 0)
            norm2_rows(0, 1)
            residual(1, 2)
            norm2_rows(1, 0)
            norm2_rows(1, 1)
            norm2_mean(2, 3)
            residual(1, 3)
            norm2_root(2, 2, 3)
            norm2_rows(2, 0)
            norm2_mean(3, 4)
            norm2_rows(2, 1)
            norm2_root(3, 3, 4)
            norm2_rows(3, 0)
            norm2_rows(3, 1)
            ada_next(len(todo))

            def tt(to, a, b, op):
                link(V.tensor_tensor(to, a, b, op))

            def by(ap, **k):
                return ap.rearrange("p (t g j) -> p t g j", t=NT, g=EG)

            def mid(ap):
                return ap.unsqueeze(2).to_broadcast([P, NT, EG, GRP])

            def last(ap):
                return ap.unsqueeze(3).to_broadcast([P, NT, EG, GRP])

            def rows4(i, lo=0):
                return route[i][:, lo:lo + NT * GRP].rearrange("p (t g) -> p t g", t=NT)

            four = lambda ap: ap.unsqueeze(2).to_broadcast([P, NT, GRP])
            tile4 = lambda i: route[i][:, 0:NT]
            desc4 = desc[:].unsqueeze(1).to_broadcast([P, NT, GRP])

            def first_max(vals, to, z):
                top = tile4(5)
                link(V.tensor_reduce(top, vals, AX_X, ALU.max))
                tt(z, vals, four(top), ALU.is_equal)
                tt(z, z, desc4, ALU.mult)
                link(V.tensor_reduce(top, z, AX_X, ALU.max))
                tt(to, z, four(top), ALU.is_equal)

            dve.wait_ge(bias_in, 16)
            dve.wait_ge(const_ok, 9)
            for t in (1, 2):
                dve.wait_ge(h2_stored[t], 16)
            s, sel = route[0], route[1]
            dve.wait_ge(score_pe, 1)
            link(V.tensor_copy(s, bank[6][:, 0:NT * E]))
            tt(sel.rearrange("p (t e) -> p t e", t=NT), s.rearrange("p (t e) -> p t e", t=NT),
               bias_bc[:].unsqueeze(1).to_broadcast([P, NT, E]), ALU.add)
            n2, n1 = NT * E // 2, NT * E // 4
            pairs = sel.rearrange("p (n two) -> p n two", two=2)
            better, worse, own = route[2][:, 0:n2], route[3][:, 0:n2], route[4][:, 0:n2]
            cross, top_own = route[4][:, n2:n2 + n1], route[4][:, n2 + n1:n2 + 2 * n1]
            tt(better, pairs[:, :, 0], pairs[:, :, 1], ALU.max)
            tt(worse, pairs[:, :, 0], pairs[:, :, 1], ALU.min)
            tt(own, better, worse, ALU.add)
            of_group = lambda ap: ap.rearrange("p (n two) -> p n two", two=2)
            tt(cross, of_group(better)[:, :, 0], of_group(better)[:, :, 1], ALU.add)
            tt(top_own, of_group(own)[:, :, 0], of_group(own)[:, :, 1], ALU.max)
            tt(route[3][:, 0:n1], cross, top_own, ALU.max)
            group = rows4(6)
            first_max(rows4(3), group, rows4(6, n1))
            tt(by(route[7]), by(sel), last(group), ALU.mult)
            best, score = rows4(9), rows4(9, n1)
            link(V.tensor_reduce(best, by(route[7]).rearrange("p t g j -> p t j g"), AX_X, ALU.add))
            one, two, z = rows4(10), rows4(10, n1), rows4(10, 2 * n1)
            first_max(best, one, z)
            link(V.scalar_tensor_tensor(out=best, in0=one, scalar=-BIG, in1=best, op0=ALU.mult, op1=ALU.add))
            first_max(best, two, z)
            tt(z, one, two, ALU.add)
            mask = route[14][:, 0:NT * E // 2].bitcast(BF16)
            V.tensor_tensor(by(mask), last(group), mid(z), ALU.mult).then_inc(mask_ok, 1)

            dve.wait_ge(rank_pe, 1)
            dve.wait_ge(mask_ok, 1)
            rank, place, counts = route[15], route[16], route[17][:, 0:E]
            link(V.scalar_tensor_tensor(out=place, in0=bank[7][:, 0:NT * E], scalar=1.0, in1=mask,
                                        op0=ALU.add, op1=ALU.mult))

            def token_numbers(b):
                for e in range(*BATCHES[b], 2):
                    q = place.rearrange("p (t e) -> p t e", t=NT)[:, :, e:e + 2]
                    ins = V.tensor_tensor(onehot[:, :, e:e + 2, :], q.unsqueeze(3).to_broadcast([P, NT, 2, P]),
                                          iota_1[:].unsqueeze(1).unsqueeze(1).to_broadcast([P, NT, 2, P]), ALU.is_equal)
                ins.then_inc(hot_ok, 1)

            def read_numbers(b):
                dve.wait_ge(idx_pe, b + 1)
                mine = slice(*BATCHES[b])
                V.tensor_copy(idx_main[:, mine], bank[7][:, mine]).then_inc(idx_ok, 1)

            def weights():
                tt(by(route[8]), by(s), last(group), ALU.mult)
                link(V.tensor_reduce(score, by(route[8]).rearrange("p t g j -> p t j g"), AX_X, ALU.add))
                low, high = rows4(11), rows4(11, n1)
                tt(low, z, desc4, ALU.mult)
                link(V.tensor_reduce(tile4(5), low, AX_X, ALU.max))
                tt(low, low, four(tile4(5)), ALU.is_equal)
                tt(high, z, low, ALU.subtract)
                tt(by(m_low), last(group), mid(low), ALU.mult)
                tt(by(m_high), last(group), mid(high), ALU.mult)
                tt(low, low, score, ALU.mult)
                tt(high, high, score, ALU.mult)
                link(V.tensor_reduce(combine[:, 0, :], low, AX_X, ALU.add))
                link(V.tensor_reduce(combine[:, 1, :], high, AX_X, ALU.add))
                tt(tile4(5), combine[:, 0, :], combine[:, 1, :], ALU.add)
                link(V.reciprocal(tile4(5), tile4(5)))
                tt(combine[:, :, :], combine[:, :, :], tile4(5).unsqueeze(1).to_broadcast([P, 2, NT]), ALU.mult)

            m_low, m_high = route[12], route[13]
            token_numbers(0)
            V.tensor_copy(rank, bank[7][:, 0:NT * E]).then_inc(rank_ev, 1)
            V.tensor_copy(counts, bank[7][:, NT * E:(NT + 1) * E]).then_inc(rank_ev, 1)
            read_numbers(0)
            token_numbers(1)
            weights()
            read_numbers(1)
            token_numbers(2)
            dve.wait_ge(rank_ev, 2)

            def tokens_low(e):
                for h in range(2):
                    dve.wait_ge(sel_ok, 2 * e + h + 1)
                    cols = slice(4 * h, 4 * h + 4)
                    V.tensor_tensor(xselT[1][:, cols, :].rearrange("p k j -> p (k j)"), bank[5 + h][:],
                                    as_f32(xselT[0][:, cols, :].rearrange("p k j -> p (k j)")),
                                    ALU.subtract).then_inc(sel_low, 1)

            def hidden(e):
                dve.wait_ge(silu_ok, e + 1)
                V.tensor_tensor(hid, bank[1][:], silu_g, ALU.mult).then_inc(hid_ok, 1)

            def rows(e, i, free):
                if free is not None:
                    dve.wait_ge(stored[i], free)
                for h in range(2):
                    dve.wait_ge(y_pe, e + 1 + (h if isinstance(e, int) and e == E - 1 else 0))
                    cols = slice(h * HALF, (h + 1) * HALF)
                    V.tensor_tensor(y_sb[i][:, cols], bank[2 + h][:], gate_bc[:, cols], ALU.mult).then_inc(y_ok, 1)

            def place_slots():
                beyond, shift, slot = route[17][:, E:2 * E], route[17][:, 2 * E:3 * E], route[18]
                link(V.tensor_scalar(beyond, counts, float(P), None, ALU.is_gt))
                for k in range(2, NT):
                    link(V.scalar_tensor_tensor(out=beyond, in0=counts, scalar=float(k * P), in1=beyond,
                                                op0=ALU.is_gt, op1=ALU.add))
                link(V.tensor_tensor_scan(over_sum[:], ones[:, 0:E], beyond, 0.0, ALU.mult, ALU.add))
                tt(shift, over_sum[:], beyond, ALU.subtract)
                tt(shift, shift, iota_e[:], ALU.subtract)
                link(V.tensor_scalar(shift, shift, float(P), float(MAIN - P), ALU.mult, ALU.add))
                wide = lambda ap: ap.unsqueeze(1).to_broadcast([P, NT, E])
                te = lambda ap: ap.rearrange("p (t e) -> p t e", t=NT)
                link(V.scalar_tensor_tensor(out=te(slot), in0=te(rank), scalar=float(P), in1=wide(shift),
                                            op0=ALU.is_ge, op1=ALU.mult))
                tt(slot, slot, rank, ALU.add)
                link(V.tensor_scalar(route[19][:, 0:E], iota_e[:], float(P), None, ALU.mult))
                tt(te(slot), te(slot), wide(route[19][:, 0:E]), ALU.add)
                for i, m in enumerate((m_low, m_high)):
                    tt(route[20], m, slot, ALU.mult)
                    link(V.tensor_reduce(over_rel[:, i, :], te(route[20]), AX_X, ALU.add))
                link(V.tensor_copy(slot_u[:], over_rel[:]))
                held = route[20][:, 0:2 * NT].rearrange("p (i t) -> p i t", i=2)
                for i in range(2):
                    link(V.tensor_scalar(held[:, i, :], over_rel[:, i, :], float((E - 1 + i) * P - 1), None, ALU.min))
                V.tensor_copy(slot_main[:], held).then_inc(slots_ok, 1)
                dve.wait_ge(slots_ok, 1)
                link(V.tensor_scalar(over_rel[:], over_rel[:], float(1 - MAIN), None, ALU.add))
                link(V.memset(over_k[:], 0.0))
                V.tensor_copy(over_n[:, 0:1], over_sum[:, E - 1:E]).then_inc(over_ok, 1)

            dve.wait_ge(gate2_ok, 2)
            tokens_low(0)

            def expert(e, odd, free, last=False):
                split_low(e, range(4, KD), *gate_up_place(e, odd))
                hidden(e)
                if not last:
                    tokens_low(e + 1)
                    split_low(e + 1, range(4), *gate_up_place(e + 1, not odd))
                if not (isinstance(e, int) and e == 0):
                    rows(e - 1, 0 if odd else 1, free)

            dve.wait_ge(gu_low, 4)
            expert(0, False, None)
            read_numbers(2)
            token_numbers(3)
            expert(1, True, None)
            read_numbers(3)
            token_numbers(4)
            expert(2, False, None)
            read_numbers(4)
            with dve.Fori(LOOP, E - 1, 2) as e:
                expert(e, True, (e - 1) * 8)
                expert(e + 1, False, (e - 1) * 8)
            expert(E - 1, True, (E - 2) * 8, last=True)
            place_slots()
            rows(E - 1, 1, (E - 2) * 8)

            STEPS = STEPS_OVER
            dve.wait_ge(over_ok, 1)
            n_over = dve.value_load(over_n[0:1, 0:1], min_val=0, max_val=MOST_OVER)
            dve.wait_ge(stored[0], 8 * E)
            with dve.If(n_over > 0):
                with dve.Fori(0, n_over) as o:
                    step = [0]

                    def olink(ins):
                        step[0] += 1
                        ins.then_inc(o_order, 1)
                        dve.wait_ge(o_order, STEPS * o + step[0])

                    olink(V.tensor_scalar(over_cmp[:], over_sum[:], over_k[:, 0:1], None, ALU.is_le))
                    olink(V.tensor_reduce(over_e, over_cmp, AX_X, ALU.add))
                    V.tensor_copy(over_n[:, 1:2], over_e).then_inc(o_pick, 1)
                    for t in range(NT):
                        olink(V.tensor_scalar(over_hot[:, t, :], iota_1[:], over_rel[:, 0, t:t + 1], None, ALU.is_equal))
                        olink(V.scalar_tensor_tensor(out=over_hot[:, t, :], in0=iota_1[:], scalar=over_rel[:, 1, t:t + 1],
                                                     in1=over_hot[:, t, :], op0=ALU.is_equal, op1=ALU.add))
                    olink(V.tensor_scalar(over_rel[:], over_rel[:], float(-P), None, ALU.add))
                    olink(V.tensor_scalar(over_k[:], over_k[:], 1.0, None, ALU.add))
                    dve.wait_ge(o_idx_pe, o + 1)
                    V.tensor_copy(idx_over[:, 0:1], bank[7][:, 0:1]).then_inc(o_idx, 1)
                    dve.wait_ge(o_silu, o + 1)
                    V.tensor_tensor(hid, bank[1][:], silu_g, ALU.mult).then_inc(o_hid, 1)
                    dve.wait_ge(o_y_pe, o + 1)
                    for h in range(2):
                        cols = slice(h * HALF, (h + 1) * HALF)
                        V.tensor_tensor(y_sb[0][:, cols], bank[2 + h][:], gate_bc[:, cols], ALU.mult).then_inc(o_y, 1)
                    dve.wait_ge(o_stored, 16 * o + 16)
                    assert step[0] == STEPS
                dve.wait_ge(again, 32 * NT)

            def combine_rows(t, i):
                dve.wait_ge((low_in, high_in)[i][t], 16)
                if i:
                    dve.wait_ge(low_rows, t + 1)
                V.scalar_tensor_tensor(out=x_sb[:, t, :], in0=(y_low, y_high)[i][t], scalar=combine[:, i, t:t + 1],
                                       in1=x_sb[:, t, :], op0=ALU.mult,
                                       op1=ALU.add).then_inc((low_rows, all_rows)[i], 1)

            def final_stat(pair):
                dve.wait_ge(fin_sq, 2 * pair + 2)
                mean_square(slice(2 * pair, 2 * pair + 2), fin_stat)

            def final_rows(pair):
                dve.wait_ge(fin_stat, pair + 1)
                dve.wait_ge(fin_root, pair + 1)
                inverse_root(slice(2 * pair, 2 * pair + 2), fin_rstd)
                dve.wait_ge(fin_rstd, pair + 1)
                dve.wait_ge(final_in, 16)
                for n in range(4 * pair, 4 * pair + 4):
                    t, cols = n // 2, slice(n % 2 * HALF, (n % 2 + 1) * HALF)
                    V.scalar_tensor_tensor(out=res[t][:, cols], in0=x_sb[:, t, cols], scalar=stat[:, 2, t:t + 1],
                                           in1=final_bc[:, cols], op0=ALU.mult, op1=ALU.mult).then_inc(res_ok, 1)

            for t in range(NT):
                combine_rows(t, 0)
            for t in range(2):
                combine_rows(t, 1)
            final_stat(0)
            for t in range(2, NT):
                combine_rows(t, 1)
            final_rows(0)
            final_stat(1)
            final_rows(1)

        @block.tensor
        def _(pe):
            mm = nc.tensor.matmul
            pe.wait_ge(const_ok, 1)
            pe.wait_ge(prm_in, 64)
            nc.tensor.transpose(bank[7][:, 0:32], prm[:, :], ident[0:32, 0:32]).then_inc(prmT_pe, 1)
            pe.wait_ge(xn_ok, NT)
            pe.wait_ge(prmT_ok, 1)
            for k in range(KD):
                for t in range(NT):
                    last = nc.tensor.transpose(bank[k][:, t * P:(t + 1) * P],
                                               yflat[:, t * D + k * P:t * D + (k + 1) * P], ident[:])
                last.then_inc(xT_pe, 1)
            pe.wait_ge(const_ok, 2)
            pe.wait_ge(xT_ok, KD)
            for j in range(2):
                pe.wait_ge(ada_ok, 8 * (j + 1))
                for k in range(KD):
                    last = mm(bank[7][:, j * KD + k:j * KD + k + 1], acc[:, j, k * P:(k + 1) * P], ones[:, 0:1],
                              start=True, stop=True)
                last.then_inc(acc_used, 1)

            def pool_map(g):
                pe.wait_ge(pooled_ok, g + 1)
                if g == 0:
                    pe.wait_ge(poolw_in, 16)
                if g >= 2:
                    pe.wait_ge(pool_ev, g - 1)
                mm(bank[4 + g % 2][:], pool_w_sb[:, g, :], yT[:, NC + g, :], start=True, stop=True).then_inc(pool_pe, 1)

            def spread(j, b, signal):
                pe.wait_ge(ada_ok, 8 * (j + 1))
                for h in range(2):
                    last = mm(bank[b + h][:], ones[:], acc[:, j % 2, h * HALF:(h + 1) * HALF], start=True, stop=True)
                last.then_inc(signal, 1)

            for n in range(len(tiles)):
                if n >= 4:
                    pe.wait_ge(*freed[n - 4])
                for k in range(KD):
                    if k % 4 == 0:
                        b = 2 * n + k // 4
                        pe.wait_ge(lhs_low, b + 1)
                    if n == 0:
                        pe.wait_ge(rhs_low, k + 1)
                    for q, (w, h) in enumerate(((0, 0), (0, 1), (1, 0))):
                        last = mm(bank[n % 4][:], wsplit[w][:, b % 2, k % 4, :], hT[h][:, k, :],
                                  start=k == 0 and q == 0, stop=k == KD - 1 and q == 2)
                    if k % 4 == 3:
                        last.then_inc(half_done, 1)
                if 1 <= n <= NG:
                    pool_map(n - 1)
                if n in REDUCE_AFTER:
                    j = REDUCE_AFTER[n]
                    if j > 2:
                        pe.wait_ge(bc_ev, 2 * (j - 2))
                    spread(j, 6, bc_pe)

            def h2_by_channel(t):
                for k in range(KD):
                    if k % 4 == 0:
                        pe.wait_ge(h2_ok, 2 * t + k // 4 + 1)
                    last = nc.tensor.transpose(bank[4 + k // 4][:, (k % 4) * P:(k % 4 + 1) * P],
                                               h2[t][:, k * P:(k + 1) * P], ident[:])
                last.then_inc(h2T_pe, 1)

            def logits(t):
                for k in range(KD):
                    if k % 4 == 0:
                        pe.wait_ge(h2T_ok, 2 * t + k // 4 + 1)
                    last = mm(bank[6 + t // 2][0:E, t * P:(t + 1) * P], wr[:, k, :], h2T[:, k, :],
                              start=k == 0, stop=k == KD - 1)
                last.then_inc(logit_pe, 1)

            for n in range(NP, NP + NM):
                h, t = divmod(n - NP, NT)
                if h == 0:
                    pe.wait_ge(*freed[n - 4])
                else:
                    pe.wait_ge(x2_ok, n - NP - 3)
                for i in range(KD):
                    b = 2 * n + i // 4
                    if i % 4 == 0:
                        pe.wait_ge(lhs_low, b + 1)
                    if t == 0:
                        pe.wait_ge(rhs_low, KD * (1 + h) + i + 1)
                    for q, (r, w) in enumerate(((0, 0), (0, 1), (1, 0))):
                        last = mm(bank[n % 4][:], wsplit[r][:, b % 2, i % 4, :], hT[w][:, i, :],
                                  start=i == 0 and q == 0, stop=i == KD - 1 and q == 2)
                    if i % 4 == 3:
                        last.then_inc(half_done, 1)
                    if n == NP + NM - 1 and i == 3:
                        h2_by_channel(0)
            pe.wait_ge(wr_in, 16)
            pe.wait_ge(scale_ok, 2)
            for t in range(NT):
                if t:
                    h2_by_channel(t)
                logits(t)
            for t in range(NT):
                pe.wait_ge(score_ok, t // 2 + 1)
                last = nc.tensor.transpose(bank[6][:, t * E:(t + 1) * E], scoreT[:, t * P:(t + 1) * P], ident[0:E, 0:E])
            last.then_inc(score_pe, 1)
            pe.wait_ge(x2_ok, NM)
            spread(5, 0, gate2_pe)

            pe.wait_ge(mask_ok, 1)
            pe.wait_ge(const_ok, 9)
            mask = route[14][:, 0:NT * E // 2].bitcast(BF16).rearrange("p (t e) -> p t e", t=NT)
            for t in range(NT + 1):
                for q in range(min(t + 1, NT)):
                    last = mm(bank[7][:, t * E:(t + 1) * E], before[:] if q == t else ones_h[:], mask[:, q, :],
                              start=q == 0, stop=q == min(t, NT - 1))
            last.then_inc(rank_pe, 1)

            def sel(e, i, value):
                pe.wait_ge(gathered[i], value)
                for k in range(KD):
                    last = nc.tensor.transpose(bank[5 + k // 4][:, (k % 4) * P:(k % 4 + 1) * P],
                                               xg[i][:, k * P:(k + 1) * P], ident[:])
                last.then_inc(sel_pe, 1)

            def gate_up(e):
                for k in range(KD):
                    if k % 4 == 0:
                        pe.wait_ge(sel_low, 2 * e + k // 4 + 1)
                    pe.wait_ge(gu_low, 8 * e + k + 1)
                    for q, (a, w) in enumerate(((0, 0), (0, 1), (1, 0))):
                        for h in range(2):
                            last = mm(bank[h][:], xselT[a][:, k, :], wchunk[w][:, k % 4, h * F:(h + 1) * F],
                                      start=k == 0 and q == 0, stop=k == KD - 1 and q == 2)
                    last.then_inc(chunk_pe, 1)

            def down(slot, halves=(0, 1)):
                for h in halves:
                    for k in range(KF):
                        last = mm(bank[2 + h][:], hidT[:, k, :], ring_k[slot][:, k, h * HALF:(h + 1) * HALF],
                                  start=k == 0, stop=k == KF - 1)
                return last

            def hidden(e):
                pe.wait_ge(hid_ok, e + 1)
                for k in range(KF):
                    last = nc.tensor.transpose(bank[4][:, k * P:(k + 1) * P], hid[:, k * P:(k + 1) * P], ident[:])
                last.then_inc(hidT_pe, 1)

            def down_rows(e, slot, value):
                pe.wait_ge(slot_in[slot], value)
                pe.wait_ge(hidT_ok, e + 1)
                down(slot).then_inc(y_pe, 1)

            def expert(e, odd):
                h16 = 8 * (e - 1) if odd else 8 * e
                gate_up(e)
                if not (isinstance(e, int) and e == E - 1):
                    sel(e + 1, 0 if odd else 1, h16 + 32 if odd else h16 + 16)
                if not (isinstance(e, int) and e == 1):
                    pe.wait_ge(y_ok, 2 * e - 2)
                down_rows(e - 1, 2 if odd else 5, h16 + 16)
                if isinstance(e, int) and e in (1, 2):
                    numbers(e + 2)
                hidden(e)

            def numbers(b):
                pe.wait_ge(hot_ok, b + 1)
                pe.wait_ge(*((rank_ev, 2) if b == 0 else (idx_ok, b)))
                for e in range(*BATCHES[b]):
                    for t in range(NT):
                        for i in range(2):
                            last = mm(bank[7][:, e:e + 1], onehot[:, t, e, :], tok_id[:, t, i:i + 1],
                                      start=t == 0 and i == 0, stop=t == NT - 1 and i == 1)
                last.then_inc(idx_pe, 1)

            for b in range(2):
                numbers(b)
            sel(0, 0, 16)
            pe.wait_ge(gate2_ok, 2)
            gate_up(0)
            sel(1, 1, 16)
            numbers(2)
            hidden(0)
            expert(1, True)
            expert(2, False)
            with pe.Fori(LOOP, E - 1, 2) as e:
                expert(e, True)
                expert(e + 1, False)
            expert(E - 1, True)
            pe.wait_ge(y_ok, 2 * E - 2)
            pe.wait_ge(slot_in[5], 8 * (E + 2))
            pe.wait_ge(hidT_ok, E)
            for h in range(2):
                down(5, (h,)).then_inc(y_pe, 1)

            pe.wait_ge(over_ok, 1)
            n_over = pe.value_load(over_n[0:1, 0:1], min_val=0, max_val=MOST_OVER)
            with pe.If(n_over > 0):
                with pe.Fori(0, n_over) as o:
                    pe.wait_ge(o_order, STEPS_OVER * o + 2 * NT + 2)
                    for t in range(NT):
                        for i in range(2):
                            last = mm(bank[7][:, 0:1], over_hot[:, t, :], tok_id[:, t, i:i + 1],
                                      start=t == 0 and i == 0, stop=t == NT - 1 and i == 1)
                    last.then_inc(o_idx_pe, 1)
                    pe.wait_ge(o_gathered, 16 * o + 16)
                    for k in range(KD):
                        last = nc.tensor.transpose(bank[5 + k // 4][:, (k % 4) * P:(k % 4 + 1) * P],
                                                   xg[0][:, k * P:(k + 1) * P], ident[:])
                    last.then_inc(o_sel_pe, 1)
                    pe.wait_ge(o_sel, 2 * o + 2)
                    pe.wait_ge(o_w, 48 * o + 48)
                    for k in range(KD):
                        for h in range(2):
                            last = mm(bank[h][:], over_selT[:, k, :], ring_k[k // 4][:, k % 4, h * F:(h + 1) * F],
                                      start=k == 0, stop=k == KD - 1)
                    last.then_inc(o_gu, 1)
                    pe.wait_ge(o_hid, o + 1)
                    for k in range(KF):
                        last = nc.tensor.transpose(bank[4][:, k * P:(k + 1) * P], hid[:, k * P:(k + 1) * P], ident[:])
                    last.then_inc(o_hidT_pe, 1)
                    pe.wait_ge(o_hidT, o + 1)
                    down(2).then_inc(o_y_pe, 1)


_INS = ['x', 'c', 'w_in', 'conv_w', 'pool_w', 'pool_scale', 'w_out', 'norm1_g', 'norm2_g',
        'w_ada', 'b_ada', 'w_router', 'router_bias', 'w_gate_up', 'w_down', 'final_g']
_OUTS = [((1, 512, 1024), 'float32')]


def kernel(**inputs):
    import numpy as _np
    import concourse.bacc as _bacc
    from concourse import mybir as _mybir
    from concourse.bass_utils import run_bass_kernel_spmd as _run

    nc = _bacc.Bacc("TRN2", target_bir_lowering=False, num_devices=1)
    arrays, args = {}, []
    for name in _INS:
        a = _np.ascontiguousarray(inputs[name])
        arrays[f"in_{name}_dram"] = a
        args.append(nc.dram_tensor(f"in_{name}_dram", a.shape, _mybir.dt.from_np(a.dtype), kind="ExternalInput").ap())
    for i, (shape, dtype) in enumerate(_OUTS):
        dt = _mybir.dt.from_np(_np.dtype(dtype))
        args.append(nc.dram_tensor(f"out_{i}_dram", shape, dt, kind="ExternalOutput").ap())
    hybrid_block(nc, *args)
    r = _run(nc, [arrays], core_ids=[0])
    return r.results[0]["out_0_dram"]
```
